# Optimizing a Trainium2 kernel written in Bass

```python
import math
import jax
import jax.numpy as jnp
from jax import lax
import numpy as np

D_MODEL = 2048
BATCH = 1
SEQ = 256
DEPTH = 1

N_MIXERS = 4
PLE_DIM = 256
D_FF = 4 * D_MODEL
EPS = 1e-6
NEG = -1e30
FORCE_BONUS = 1e4

NSA_HEAD_DIM = 128
NSA_HEADS = D_MODEL // NSA_HEAD_DIM
NSA_KV_HEADS = NSA_HEADS // 4
NSA_CMP_STRIDE = 16
NSA_CMP_BLOCK = 2 * NSA_CMP_STRIDE
NSA_SEL_BLOCK = 64
NSA_TOP_N = 16
NSA_WINDOW = 512
NSA_Q_BLOCK = 32
NSA_IN = NSA_HEADS * NSA_HEAD_DIM + 6 * NSA_KV_HEADS * NSA_HEAD_DIM + 3 * NSA_HEADS

M2_D_INNER = 2 * D_MODEL
M2_HEAD_DIM = 64
M2_HEADS = M2_D_INNER // M2_HEAD_DIM
M2_GROUPS = 8
M2_STATE = 128
M2_CONV = 4
M2_CHUNK = 128
M2_CONV_DIM = M2_D_INNER + 2 * M2_GROUPS * M2_STATE
M2_IN = M2_D_INNER + M2_CONV_DIM + M2_HEADS

GDN_HEAD_DIM = 128
GDN_K_HEADS = D_MODEL // GDN_HEAD_DIM
GDN_V_HEADS = 2 * GDN_K_HEADS
GDN_CONV = 4
GDN_CHUNK = 64
GDN_CONV_DIM = (2 * GDN_K_HEADS + GDN_V_HEADS) * GDN_HEAD_DIM
GDN_IN = GDN_CONV_DIM + GDN_V_HEADS * GDN_HEAD_DIM + 2 * GDN_V_HEADS

ML_HEADS = 4
ML_QK_DIM = D_MODEL // (2 * ML_HEADS)
ML_V_DIM = D_MODEL // ML_HEADS
ML_CHUNK = 64
ML_IN = 2 * ML_HEADS * ML_QK_DIM + 2 * ML_HEADS * ML_V_DIM + 2 * ML_HEADS

kernel_name = 'hybrid_nsa_ssd_gdn_mlstm_trunk'

def rms_norm(x, g):
    xf = x.astype(jnp.float32)
    y = xf * lax.rsqrt(jnp.mean(xf * xf, axis=-1, keepdims=True) + EPS)
    return (y * g.astype(jnp.float32)).astype(x.dtype)

def l2_norm(x):
    xf = x.astype(jnp.float32)
    return (xf * lax.rsqrt(jnp.sum(xf * xf, axis=-1, keepdims=True) + EPS)).astype(x.dtype)

def causal_dwconv(x, w):
    k, c = w.shape
    return lax.conv_general_dilated(x, w[:, None, :].astype(x.dtype), window_strides=(1,), padding=[(k - 1, 0)], dimension_numbers=('NWC', 'WIO', 'NWC'), feature_group_count=c)

def masked_softmax(s, mask):
    s = jnp.where(mask, s.astype(jnp.float32), NEG)
    e = jnp.where(mask, jnp.exp(s - jnp.max(s, axis=-1, keepdims=True)), 0.0)
    return e / jnp.maximum(jnp.sum(e, axis=-1, keepdims=True), 1e-30)

def _to_chunks(t, L):
    bsz, seq, h = t.shape[:3]
    t = t.astype(jnp.float32).reshape((bsz, seq // L, L, h) + t.shape[3:])
    return jnp.transpose(t, (1, 0, 3, 2) + tuple(range(4, t.ndim)))

def _from_chunks(t):
    nc, bsz, h, L = t.shape[:4]
    t = jnp.transpose(t, (1, 0, 3, 2) + tuple(range(4, t.ndim)))
    return t.reshape((bsz, nc * L, h) + t.shape[4:])

def nsa_mixer(u, w_in, q_g, k_g, cmp_pos, cmp_w1, cmp_w2, w_out):
    bsz, seq, _ = u.shape
    H, G, dk = NSA_HEADS, NSA_KV_HEADS, NSA_HEAD_DIM
    hpg = H // G
    L, STR, SEL, W, QB = NSA_CMP_BLOCK, NSA_CMP_STRIDE, NSA_SEL_BLOCK, NSA_WINDOW, NSA_Q_BLOCK
    n_cmp = seq // STR - 1
    n_sel = seq // SEL
    n_top = min(NSA_TOP_N, n_sel)
    nq = seq // QB
    scale = dk ** -0.5
    splits = [int(v) for v in np.cumsum([H * dk] + [G * dk] * 6)]
    q, k_c, v_c, k_s, v_s, k_w, v_w, gate = jnp.split(u @ w_in, splits, axis=-1)

    def kv(t):
        return t.reshape(bsz, seq, G, dk)

    q = rms_norm(q.reshape(bsz, seq, H, dk), q_g)
    gate = jax.nn.sigmoid(gate.reshape(bsz, seq, H, 3))

    def compress(t, pos, w1, w2):
        ch = t.reshape(bsz, seq // STR, STR, G, dk)
        blk = jnp.concatenate([ch[:, :-1], ch[:, 1:]], axis=2) + pos[:, None, :]
        return jax.nn.silu(jnp.einsum('bnlgd,lde->bnge', blk, w1)) @ w2

    k_c = rms_norm(compress(kv(k_c), cmp_pos[0], cmp_w1[0], cmp_w2[0]), k_g[0])
    v_c = compress(kv(v_c), cmp_pos[1], cmp_w1[1], cmp_w2[1])
    k_s = rms_norm(kv(k_s), k_g[1]).reshape(bsz, n_sel, SEL, G, dk).transpose(0, 3, 1, 2, 4)
    v_s = kv(v_s).reshape(bsz, n_sel, SEL, G, dk).transpose(0, 3, 1, 2, 4)
    pad = ((0, 0), (W, 0), (0, 0), (0, 0))
    k_w = jnp.pad(rms_norm(kv(k_w), k_g[2]), pad)
    v_w = jnp.pad(kv(v_w), pad)

    c_start = jnp.arange(n_cmp) * STR
    c_end = c_start + L - 1
    s_start = jnp.arange(n_sel) * SEL
    overlap = ((c_start[:, None] < s_start[None, :] + SEL) & (c_end[:, None] >= s_start[None, :])).astype(jnp.float32)
    blk_id = jnp.arange(n_sel)
    take = jax.vmap(jax.vmap(lambda tab, ix: tab[ix]))

    def block(args):
        qb, gb, s0 = args
        t = s0 + jnp.arange(QB)
        sc = jnp.einsum('bghqd,bngd->bghqn', qb, k_c) * scale
        pc = masked_softmax(sc, c_end[None, :] <= t[:, None])
        o_cmp = jnp.einsum('bghqn,bngd->bghqd', pc.astype(v_c.dtype), v_c)
        imp = jnp.einsum('bgqn,nj->bgqj', pc.sum(axis=2), overlap)
        cur = t // SEL
        forced = (blk_id[None, :] == 0) | (blk_id[None, :] == cur[:, None]) | (blk_id[None, :] == cur[:, None] - 1)
        imp = jnp.where(blk_id[None, :] <= cur[:, None], imp + jnp.where(forced, FORCE_BONUS, 0.0), NEG)
        _, idx = lax.top_k(imp, n_top)
        kg = take(k_s, idx).reshape(bsz, G, QB, n_top * SEL, dk)
        vg = take(v_s, idx).reshape(bsz, G, QB, n_top * SEL, dk)
        kpos = (idx[..., None] * SEL + jnp.arange(SEL)).reshape(bsz, G, QB, n_top * SEL)
        ss = jnp.einsum('bghqd,bgqkd->bghqk', qb, kg) * scale
        ps = masked_softmax(ss, (kpos <= t[:, None])[:, :, None])
        o_slc = jnp.einsum('bghqk,bgqkd->bghqd', ps.astype(vg.dtype), vg)
        kwb = lax.dynamic_slice_in_dim(k_w, s0, W + QB, axis=1)
        vwb = lax.dynamic_slice_in_dim(v_w, s0, W + QB, axis=1)
        wpos = s0 - W + jnp.arange(W + QB)
        mw = (wpos[None, :] <= t[:, None]) & (wpos[None, :] > t[:, None] - W) & (wpos[None, :] >= 0)
        sw = jnp.einsum('bghqd,bkgd->bghqk', qb, kwb) * scale
        o_win = jnp.einsum('bghqk,bkgd->bghqd', masked_softmax(sw, mw).astype(vwb.dtype), vwb)
        return gb[..., 0:1] * o_cmp + gb[..., 1:2] * o_slc + gb[..., 2:3] * o_win

    q_blk = q.reshape(bsz, nq, QB, G, hpg, dk).transpose(1, 0, 3, 4, 2, 5)
    g_blk = gate.reshape(bsz, nq, QB, G, hpg, 3).transpose(1, 0, 3, 4, 2, 5)
    o = lax.map(block, (q_blk, g_blk, jnp.arange(nq) * QB))
    o = o.transpose(1, 0, 4, 2, 3, 5).reshape(bsz, seq, H * dk)
    return o @ w_out

def ssd_chunked(x, dt, a, bm, cm):
    bsz, seq, g, r, p = x.shape
    n = bm.shape[-1]
    L = M2_CHUNK

    def chunks(t):
        return t.astype(jnp.float32).reshape((bsz, seq // L, L) + t.shape[2:]).swapaxes(0, 1)

    causal = jnp.tril(jnp.ones((L, L), bool))[None, :, :, None, None]

    def step(state, inp):
        xc, lac, bc, cc = inp
        cum = jnp.cumsum(lac, axis=1)
        decay = jnp.exp(jnp.where(causal, cum[:, :, None] - cum[:, None], -jnp.inf))
        cb = jnp.einsum('btgn,bsgn->btsg', cc, bc)
        y = jnp.einsum('btsg,btsgr,bsgrp->btgrp', cb, decay, xc)
        y = y + jnp.einsum('btgn,bgrpn->btgrp', cc, state) * jnp.exp(cum)[..., None]
        tail = jnp.exp(cum[:, -1:] - cum)
        state = state * jnp.exp(cum[:, -1])[..., None, None] + jnp.einsum('bsgr,bsgrp,bsgn->bgrpn', tail, xc, bc)
        return state, y

    state0 = jnp.zeros((bsz, g, r, p, n), jnp.float32)
    _, y = lax.scan(step, state0, (chunks(x * dt[..., None]), chunks(dt * a), chunks(bm), chunks(cm)))
    return y.swapaxes(0, 1).reshape(bsz, seq, g, r, p)

def mamba2_mixer(u, w_in, conv_w, conv_b, dt_bias, a_log, d_skip, norm_g, w_out):
    bsz, seq, _ = u.shape
    Di, H, P, G, N = M2_D_INNER, M2_HEADS, M2_HEAD_DIM, M2_GROUPS, M2_STATE
    R = H // G
    z, xbc, dt = jnp.split(u @ w_in, [Di, Di + M2_CONV_DIM], axis=-1)
    xbc = jax.nn.silu(causal_dwconv(xbc, conv_w) + conv_b)
    xs, bm, cm = jnp.split(xbc, [Di, Di + G * N], axis=-1)
    dt = jax.nn.softplus((dt + dt_bias).astype(jnp.float32)).reshape(bsz, seq, G, R)
    a = -jnp.exp(a_log.astype(jnp.float32)).reshape(G, R)
    xs = xs.reshape(bsz, seq, G, R, P)
    y = ssd_chunked(xs, dt, a, bm.reshape(bsz, seq, G, N), cm.reshape(bsz, seq, G, N))
    y = y + d_skip.reshape(G, R, 1) * xs
    y = (y * jax.nn.silu(z).reshape(bsz, seq, G, R, P)).reshape(bsz, seq, G, Di // G)
    y = rms_norm(y, norm_g.reshape(G, Di // G)).reshape(bsz, seq, Di)
    return y @ w_out

def gated_delta_chunked(q, k, v, beta, g):
    L = GDN_CHUNK
    bsz, seq, h, dk = k.shape
    dv = v.shape[-1]
    incl = jnp.tril(jnp.ones((L, L), bool))
    strict = jnp.tril(jnp.ones((L, L), bool), -1)
    eye = jnp.eye(L, dtype=jnp.float32)

    def step(state, inp):
        qc, kc, vc, bc, gc = inp
        cum = jnp.cumsum(gc, axis=-1)
        dmask = jnp.exp(jnp.where(incl, cum[..., :, None] - cum[..., None, :], -jnp.inf))
        kb = kc * bc[..., None]
        tri = eye + jnp.where(strict, jnp.einsum('bhid,bhjd->bhij', kb, kc) * dmask, 0.0)
        rhs = jnp.concatenate([vc * bc[..., None], kb * jnp.exp(cum)[..., None]], axis=-1)
        sol = lax.linalg.triangular_solve(tri, rhs, left_side=True, lower=True, unit_diagonal=True)
        v_new = sol[..., :dv] - jnp.einsum('bhik,bhkv->bhiv', sol[..., dv:], state)
        attn = jnp.einsum('bhid,bhjd->bhij', qc, kc) * dmask
        o = jnp.einsum('bhik,bhkv->bhiv', qc * jnp.exp(cum)[..., None], state) + jnp.einsum('bhij,bhjv->bhiv', attn, v_new)
        state = state * jnp.exp(cum[..., -1])[..., None, None] + jnp.einsum('bhik,bhiv->bhkv', kc * jnp.exp(cum[..., -1:] - cum)[..., None], v_new)
        return state, o

    state0 = jnp.zeros((bsz, h, dk, dv), jnp.float32)
    _, o = lax.scan(step, state0, (_to_chunks(q, L), _to_chunks(k, L), _to_chunks(v, L), _to_chunks(beta, L), _to_chunks(g, L)))
    return _from_chunks(o)

def gdn_mixer(u, w_in, conv_w, a_log, dt_bias, norm_g, w_out):
    bsz, seq, _ = u.shape
    Hk, Hv, dh = GDN_K_HEADS, GDN_V_HEADS, GDN_HEAD_DIM
    qkv, z, b, a = jnp.split(u @ w_in, [GDN_CONV_DIM, GDN_CONV_DIM + Hv * dh, GDN_CONV_DIM + Hv * dh + Hv], axis=-1)
    qkv = jax.nn.silu(causal_dwconv(qkv, conv_w))
    q, k, v = jnp.split(qkv, [Hk * dh, 2 * Hk * dh], axis=-1)
    rep = Hv // Hk
    q = jnp.repeat(l2_norm(q.reshape(bsz, seq, Hk, dh)) * dh ** -0.5, rep, axis=2)
    k = jnp.repeat(l2_norm(k.reshape(bsz, seq, Hk, dh)), rep, axis=2)
    beta = jax.nn.sigmoid(b.astype(jnp.float32))
    g = -jnp.exp(a_log.astype(jnp.float32)) * jax.nn.softplus((a + dt_bias).astype(jnp.float32))
    o = gated_delta_chunked(q, k, v.reshape(bsz, seq, Hv, dh), beta, g)
    o = rms_norm(o, norm_g) * jax.nn.silu(z.reshape(bsz, seq, Hv, dh))
    return o.reshape(bsz, seq, Hv * dh) @ w_out

def mlstm_chunked(q, k, v, li, lf):
    L = ML_CHUNK
    bsz, seq, h, dq = q.shape
    dv = v.shape[-1]
    incl = jnp.tril(jnp.ones((L, L), bool))

    def step(carry, inp):
        c, n, m = carry
        qc, kc, vc, lic, lfc = inp
        b = jnp.cumsum(lfc, axis=-1)
        dlog = jnp.where(incl, b[..., :, None] - b[..., None, :] + lic[..., None, :], -jnp.inf)
        inter = b + m[..., None]
        m_t = jnp.maximum(inter, jnp.max(dlog, axis=-1))
        w_inter = jnp.exp(inter - m_t)
        s = jnp.einsum('bhtd,bhsd->bhts', qc, kc) * jnp.exp(dlog - m_t[..., None])
        num = jnp.einsum('bhts,bhsv->bhtv', s, vc) + w_inter[..., None] * jnp.einsum('bhtd,bhdv->bhtv', qc, c)
        den = jnp.sum(s, axis=-1) + w_inter * jnp.einsum('bhtd,bhd->bht', qc, n)
        hc = num / jnp.maximum(jnp.abs(den), jnp.exp(-m_t))[..., None]
        tot = b[..., -1]
        ulog = tot[..., None] - b + lic
        m_new = jnp.maximum(tot + m, jnp.max(ulog, axis=-1))
        wu = jnp.exp(ulog - m_new[..., None])
        dec = jnp.exp(tot + m - m_new)
        c = dec[..., None, None] * c + jnp.einsum('bhs,bhsd,bhsv->bhdv', wu, kc, vc)
        n = dec[..., None] * n + jnp.einsum('bhs,bhsd->bhd', wu, kc)
        return (c, n, m_new), hc

    carry0 = (jnp.zeros((bsz, h, dq, dv), jnp.float32), jnp.zeros((bsz, h, dq), jnp.float32), jnp.zeros((bsz, h), jnp.float32))
    _, hs = lax.scan(step, carry0, (_to_chunks(q, L), _to_chunks(k, L), _to_chunks(v, L), _to_chunks(li, L), _to_chunks(lf, L)))
    return _from_chunks(hs)

def mlstm_mixer(u, w_in, gate_b, norm_g, w_out):
    bsz, seq, _ = u.shape
    H, dq, dv = ML_HEADS, ML_QK_DIM, ML_V_DIM
    q, k, v, o, gi = jnp.split(u @ w_in, [H * dq, 2 * H * dq, 2 * H * dq + H * dv, 2 * H * dq + 2 * H * dv], axis=-1)
    gi = (gi + gate_b).astype(jnp.float32)
    hh = mlstm_chunked(q.reshape(bsz, seq, H, dq) * dq ** -0.5, k.reshape(bsz, seq, H, dq), v.reshape(bsz, seq, H, dv), gi[..., :H], jax.nn.log_sigmoid(gi[..., H:]))
    hh = rms_norm(hh, norm_g.reshape(H, dv)).reshape(bsz, seq, H * dv)
    return (jax.nn.sigmoid(o) * hh) @ w_out

def setup_inputs(seed: int = 0) -> dict:
    key = jax.random.key(seed)
    keys = iter(jax.random.split(key, 48))
    f32 = jnp.float32
    D = D_MODEL
    res = (2 * DEPTH) ** -0.5

    def normal(shape, std):
        return jax.random.normal(next(keys), shape, f32) * std

    def gain(shape):
        return 1.0 + 0.02 * jax.random.normal(next(keys), shape, f32)

    def unif(shape, lo, hi):
        return jax.random.uniform(next(keys), shape, f32, lo, hi)

    def dt_bias(shape):
        dt = jnp.exp(unif(shape, math.log(1e-3), math.log(1e-1)))
        return dt + jnp.log(-jnp.expm1(-dt))

    n_a, n_b, n_c, n_d = [len(range(m, DEPTH, N_MIXERS)) for m in range(N_MIXERS)]
    dk = NSA_HEAD_DIM
    return {
        'x': normal((BATCH, SEQ, D), 1.0),
        'p': normal((DEPTH, BATCH, SEQ, PLE_DIM), 1.0),
        'norm_mix_g': gain((DEPTH, D)),
        'norm_mlp_g': gain((DEPTH, D)),
        'mlp_w1': normal((DEPTH, D, D_FF), D ** -0.5),
        'mlp_w2': normal((DEPTH, D_FF, D), res * D_FF ** -0.5),
        'ple_norm_g': gain((DEPTH, D)),
        'ple_w_gate': normal((DEPTH, D, D), D ** -0.5),
        'ple_w_proj': normal((DEPTH, PLE_DIM, D), res * PLE_DIM ** -0.5),
        'nsa_w_in': normal((n_a, D, NSA_IN), D ** -0.5),
        'nsa_q_g': gain((n_a, dk)),
        'nsa_k_g': gain((n_a, 3, dk)),
        'nsa_cmp_pos': normal((n_a, 2, NSA_CMP_BLOCK, dk), 0.02),
        'nsa_cmp_w1': normal((n_a, 2, NSA_CMP_BLOCK, dk, dk), (NSA_CMP_BLOCK * dk) ** -0.5),
        'nsa_cmp_w2': normal((n_a, 2, dk, dk), dk ** -0.5),
        'nsa_w_out': normal((n_a, NSA_HEADS * dk, D), res * (NSA_HEADS * dk) ** -0.5),
        'm2_w_in': normal((n_b, D, M2_IN), D ** -0.5),
        'm2_conv_w': normal((n_b, M2_CONV, M2_CONV_DIM), M2_CONV ** -0.5),
        'm2_conv_b': normal((n_b, M2_CONV_DIM), 0.02),
        'm2_dt_bias': dt_bias((n_b, M2_HEADS)),
        'm2_a_log': jnp.log(unif((n_b, M2_HEADS), 1.0, 16.0)),
        'm2_d': gain((n_b, M2_HEADS)),
        'm2_norm_g': gain((n_b, M2_D_INNER)),
        'm2_w_out': normal((n_b, M2_D_INNER, D), res * M2_D_INNER ** -0.5),
        'gdn_w_in': normal((n_c, D, GDN_IN), D ** -0.5),
        'gdn_conv_w': normal((n_c, GDN_CONV, GDN_CONV_DIM), GDN_CONV ** -0.5),
        'gdn_a_log': jnp.log(unif((n_c, GDN_V_HEADS), 1.0, 16.0)),
        'gdn_dt_bias': dt_bias((n_c, GDN_V_HEADS)),
        'gdn_norm_g': gain((n_c, GDN_HEAD_DIM)),
        'gdn_w_out': normal((n_c, GDN_V_HEADS * GDN_HEAD_DIM, D), res * (GDN_V_HEADS * GDN_HEAD_DIM) ** -0.5),
        'ml_w_in': normal((n_d, D, ML_IN), D ** -0.5),
        'ml_gate_b': jnp.concatenate([normal((n_d, ML_HEADS), 0.1), unif((n_d, ML_HEADS), 3.0, 6.0)], axis=-1),
        'ml_norm_g': gain((n_d, ML_HEADS * ML_V_DIM)),
        'ml_w_out': normal((n_d, ML_HEADS * ML_V_DIM, D), res * (ML_HEADS * ML_V_DIM) ** -0.5),
    }

def reference(x, p, norm_mix_g, norm_mlp_g, mlp_w1, mlp_w2, ple_norm_g, ple_w_gate, ple_w_proj, nsa_w_in, nsa_q_g, nsa_k_g, nsa_cmp_pos, nsa_cmp_w1, nsa_cmp_w2, nsa_w_out, m2_w_in, m2_conv_w, m2_conv_b, m2_dt_bias, m2_a_log, m2_d, m2_norm_g, m2_w_out, gdn_w_in, gdn_conv_w, gdn_a_log, gdn_dt_bias, gdn_norm_g, gdn_w_out, ml_w_in, ml_gate_b, ml_norm_g, ml_w_out):
    h = x
    for i in range(DEPTH):
        kind, j = i % N_MIXERS, i // N_MIXERS
        u = rms_norm(h, norm_mix_g[i])
        if kind == 0:
            mix = nsa_mixer(u, nsa_w_in[j], nsa_q_g[j], nsa_k_g[j], nsa_cmp_pos[j], nsa_cmp_w1[j], nsa_cmp_w2[j], nsa_w_out[j])
        elif kind == 1:
            mix = mamba2_mixer(u, m2_w_in[j], m2_conv_w[j], m2_conv_b[j], m2_dt_bias[j], m2_a_log[j], m2_d[j], m2_norm_g[j], m2_w_out[j])
        elif kind == 2:
            mix = gdn_mixer(u, gdn_w_in[j], gdn_conv_w[j], gdn_a_log[j], gdn_dt_bias[j], gdn_norm_g[j], gdn_w_out[j])
        else:
            mix = mlstm_mixer(u, ml_w_in[j], ml_gate_b[j], ml_norm_g[j], ml_w_out[j])
        h = h + mix
        u = rms_norm(h, norm_mlp_g[i])
        h = h + jnp.square(jax.nn.relu(u @ mlp_w1[i])) @ mlp_w2[i]
        gate = jax.nn.sigmoid(rms_norm(h, ple_norm_g[i]) @ ple_w_gate[i])
        h = h + gate * (p[i] @ ple_w_proj[i])
    return h


_drawn_inputs = setup_inputs


def setup_inputs(seed=0):
    import zlib

    import numpy as np

    out = dict(_drawn_inputs(seed))
    spreads = {}
    factors = {'norm_mix_g': 8.0,
     'norm_mlp_g': 11.115,
     'ple_norm_g': 200.0,
     'nsa_q_g': 8.0,
     'nsa_k_g': 8.0,
     'nsa_cmp_pos': 8.0,
     'ple_w_gate': 21.712,
     'p': 8.0,
     'ple_w_proj': 8.0}
    for name, (base, spread) in spreads.items():
        noise = np.random.default_rng([zlib.crc32(name.encode()), seed]).standard_normal(out[name].shape)
        drawn = base * np.exp(spread * noise) if base else spread * noise
        out[name] = jnp.asarray(drawn.astype(out[name].dtype))
    for name, factor in factors.items():
        out[name] = (out[name] * factor).astype(out[name].dtype)
    return out
```

```python
from contextlib import ExitStack

import numpy as np

import concourse.bass as bass
from concourse import mybir

F32 = mybir.dt.float32
F32R = mybir.dt.float32r
ACT = mybir.ActivationFunctionType
ALU = mybir.AluOpType
AXX = mybir.AxisListType.X

P = 128
D = 2048
SEQ = 256
TT = SEQ // P
KT = D // P
NW = 512
UNIT_KT = 2
UW = UNIT_KT * NW
UPC = KT // UNIT_KT
RAW = 8
SPLIT = 4
H, G, DK = 16, 4, 128
HPG = H // G
QKV = H * DK
GATES = 3 * H
N_CMP = SEQ // 16 - 1
CL = 32
CMP_UNITS = CL * DK // UW
D_FF = 4 * D
QUARTERS = 4
PLE = 256
EPS = 1e-6
NEG = -1e30
SCALE = DK ** -0.5

C_KC, C_VC, C_KS, C_KW, C_VS, C_VW, C_GATE, C_Q = range(8)
C_OUT = C_Q + G
C_MLP = C_OUT + 4
C_PLE = C_MLP + 8 * QUARTERS
W_IN_COL = {C_KC: QKV, C_VC: QKV + NW, C_KS: QKV + 2 * NW, C_VS: QKV + 3 * NW, C_KW: QKV + 4 * NW,
            C_VW: QKV + 5 * NW, C_GATE: QKV + 6 * NW}
W_IN_COL.update({C_Q + g: g * NW for g in range(G)})

FIRST, END, CMP_FIRST = {}, {}, {}


def _number_units():
    u = 0
    for c in range(C_OUT):
        FIRST[c] = u
        u += 1 if c == C_GATE else UPC
        END[c] = u
        if c in (C_KS, C_KW):
            CMP_FIRST[c - C_KS] = u
            u += CMP_UNITS
    FIRST[C_OUT], END[C_OUT], END[C_OUT + 1] = u, u + 2 * UPC - 1, u + 2 * UPC
    u += 2 * UPC
    for c in (C_OUT + 2, C_OUT + 3, *range(C_MLP, C_PLE)):
        FIRST[c], END[c] = u, u + UPC
        u += UPC
    for c in range(C_PLE, C_PLE + 4):
        FIRST[c], END[c] = u, u + 1 + UPC
        u += 1 + UPC


_number_units()


def pair_order():
    first = [(n, k) for n in range(2) for k in range(UPC - 2)]
    return first + [(n, k) for k in (UPC - 2, UPC - 1) for n in range(2)]


R_X, R_KC, R_VC, R_KS, R_KW, R_P = 0, 4, 5, 6, 7, 8


def q_set(g):
    return R_P + 5 * g if g else R_P + 1


def p_set(h):
    return R_P + 1 + h + min((h + 1) // HPG + 1, G)


R_H1 = p_set(H - 1) + 1
R_MLP = R_H1 + 4
R_H2 = R_MLP + 4 * QUARTERS


def hi_sets(r):
    return r + 1 if r < R_X + 4 else 5 if r == R_P else r - R_H1 + 6



GAIN_MIX, GAIN_MLP, GAIN_PLE, GAIN_Q, GAIN_K, POS = 0, KT, 2 * KT, 3 * KT, 3 * KT + 1, 3 * KT + 4
N_CONST = POS + 2 * CL


def trunk_layer(nc, x, p, norm_mix_g, norm_mlp_g, mlp_w1, mlp_w2, ple_norm_g, ple_w_gate, ple_w_proj,
                nsa_w_in, nsa_q_g, nsa_k_g, nsa_cmp_pos, nsa_cmp_w1, nsa_cmp_w2, nsa_w_out, out):
    ctx = ExitStack()
    with ctx:
        def sb(name, shape, dt=F32):
            return ctx.enter_context(nc.sbuf_tensor(name, shape, dt))

        def pb(name):
            return ctx.enter_context(nc.psum_tensor(name, [P, NW], F32))

        def sem(name):
            return ctx.enter_context(nc.semaphore(name))

        h = sb("h", [P, TT, D])
        a_hi = sb("a_hi", [P, KT, SEQ], F32R)
        a_lo = sb("a_lo", [P, KT, SEQ], F32R)
        b_hi = sb("b_hi", [P, KT, SEQ], F32R)
        b_lo = sb("b_lo", [P, KT, SEQ], F32R)
        w_raw = sb("w_raw", [P, RAW, UW])
        w_hi = sb("w_hi", [P, SPLIT, UW], F32R)
        w_lo = sb("w_lo", [P, SPLIT, UW], F32R)
        k_t = sb("k_t", [P, G, TT, 2, P])
        v_slc = sb("v_slc", [P, TT, NW])
        v_win = sb("v_win", [P, TT, NW])
        kc_t = sb("kc_t", [P, G, N_CMP])
        v_cmp = sb("v_cmp", [N_CMP, NW])
        kc_rows = sb("kc_rows", [N_CMP, NW])
        kc_sq = sb("kc_sq", [N_CMP, NW])
        q_t = sb("q_t", [P, HPG, SEQ])
        stage = sb("stage", [P, TT, NW])
        junk = sb("junk", [P, 2 * NW])
        junk_act = sb("junk_act", [P, NW])
        s1 = sb("s1", [P, 2, 2, SEQ])
        s0 = sb("s0", [P, 2, 2, P])
        p_t = sb("p_t", [P, 2, 2 * NW])
        mx = sb("mx", [P, 2, 4])
        nmx = sb("nmx", [P, 2, 4])
        sm = sb("sm", [P, 2, 4])
        cf = sb("cf", [P, 2, 4])
        cmp_s = sb("cmp_s", [P, TT, HPG, N_CMP])
        cmp_p = sb("cmp_p", [P, 2, TT, HPG, N_CMP])
        cmp_m = sb("cmp_m", [P, TT * HPG])
        cmp_c = sb("cmp_c", [P, TT * HPG])
        gates = sb("gates", [P, TT, GATES])
        hid_e = sb("hid_e", [P, 4 * N_CMP])
        hid = sb("hid", [P, 4 * N_CMP])
        cmp_w2 = sb("cmp_w2", [P, 2, DK])
        ident = sb("ident", [P, P])
        causal = sb("causal", [P, SEQ])
        cmp_neg = sb("cmp_neg", [P, TT, N_CMP])
        cmp_one = sb("cmp_one", [P, TT, N_CMP])
        const_rows = sb("const_rows", [N_CONST, P])
        const_t = sb("const_t", [P, N_CONST])
        ss = sb("ss", [P, 3, TT, 4])
        ms = sb("ms", [P, 8])
        rs8 = sb("rs8", [P, 8])
        minus_half = sb("minus_half", [P, 8])
        rstd = sb("rstd", [P, 3, TT])
        neg_rstd = sb("neg_rstd", [P, TT])
        head_sums = sb("head_sums", [P, 8])
        p_rows = sb("p_rows", [P, TT, PLE])
        pt_hi = sb("pt_hi", [P, 2, SEQ], F32R)
        pt_lo = sb("pt_lo", [P, 2, SEQ], F32R)

        acc = [[pb(f"acc{c}{t}") for t in range(TT)] for c in range(2)]
        sc = [pb("sc0"), pb("sc1")]
        tr = [pb("tr0"), pb("tr1")]

        raw_full = [sem(f"raw_full{n}") for n in range(RAW)]
        x_full = [sem(f"x_full{n}") for n in range(4)]
        const_full = sem("const_full")
        cmp_w2_full = sem("cmp_w2_full")
        p_full = sem("p_full")
        out_stored = sem("out_stored")
        hi_done = sem("hi_done")
        lo_done = sem("lo_done")
        unit_used = sem("unit_used")
        acc_read = [[sem(f"acc_read{c}{t}") for t in range(TT)] for c in range(2)]
        tr_full = [sem(f"tr_full{b}") for b in range(2)]
        tr_hi = [sem(f"tr_hi{b}") for b in range(2)]
        tr_done = [sem(f"tr_done{b}") for b in range(2)]
        set_up = sem("set_up")
        act_step = sem("act_step")
        dve_step = sem("dve_step")
        consts_in_psum = sem("consts_in_psum")
        consts_ready = sem("consts_ready")
        sums_ready = sem("sums_ready")
        ms_ready = sem("ms_ready")
        rs_ready = sem("rs_ready")
        neg_ready = sem("neg_ready")
        normed = sem("normed")
        pos_added = sem("pos_added")
        pos_hi = sem("pos_hi")
        pos_split = sem("pos_split")
        hid_exp = sem("hid_exp")
        hid_ready = sem("hid_ready")
        kc_full = sem("kc_full")
        kc_copied = sem("kc_copied")
        kc_normed = sem("kc_normed")
        kct_full = sem("kct_full")
        kct_ready = sem("kct_ready")
        vc_full = sem("vc_full")
        vc_ready = sem("vc_ready")
        gates_ready = sem("gates_ready")
        s_full = sem("s_full")
        s_read = sem("s_read")
        s_exp = sem("s_exp")
        s_scaled = sem("s_scaled")
        cmp_full = sem("cmp_full")
        cmp_read = sem("cmp_read")
        cmp_exp = sem("cmp_exp")
        cmp_ready = sem("cmp_ready")
        o_full = sem("o_full")
        o_hi = sem("o_hi")
        o_done = sem("o_done")
        squared = sem("squared")
        out_ready = sem("out_ready")

        block = ctx.enter_context(nc.Block())

        def f32(ap):
            return ap.bitcast(F32)

        def flat(x, kt0, n):
            return x[:, kt0:kt0 + n].rearrange("p k s -> p (k s)")

        @block.sync
        def _(sp):
            def load(u, src, dst, i=0):
                if not (isinstance(i, int) and u < RAW):
                    sp.wait_ge(lo_done, u - RAW + 1 + i)
                sp.dma_start(dst, src).then_inc(raw_full[u % RAW], 16)

            def slot(u, kts=UNIT_KT, n=NW):
                return w_raw[:, u % RAW, 0:kts * n].rearrange("p (k n) -> p k n", n=n)

            def rows(w):
                return w[0].rearrange("(t p) n -> p t n", p=P)

            w_in, w_out = rows(nsa_w_in), rows(nsa_w_out)
            x_v = x[0].rearrange("(t p) d -> p t d", p=P)
            sp.dma_start(h[:, :, 0:NW], x_v[:, :, 0:NW]).then_inc(x_full[0], 16)
            for c in range(C_OUT):
                col = W_IN_COL[c]
                if c == C_GATE:
                    u = FIRST[c]
                    with nc.allow_non_contiguous_dma(reason="gate columns, 192 bytes a row"):
                        load(u, w_in[:, :, col:col + GATES], slot(u, KT, GATES))
                    continue
                for k in range(UPC):
                    u = FIRST[c] + k
                    load(u, w_in[:, UNIT_KT * k:UNIT_KT * (k + 1), col:col + NW], slot(u))
                    if c == 0 and k < 3:
                        n = k + 1
                        sp.dma_start(h[:, :, n * NW:(n + 1) * NW],
                                     x_v[:, :, n * NW:(n + 1) * NW]).then_inc(x_full[n], 16)
                if c in (C_KS, C_KW):
                    kv = c - C_KS
                    per = CL // CMP_UNITS
                    for k in range(CMP_UNITS):
                        u = CMP_FIRST[kv] + k
                        load(u, nsa_cmp_w1[0, kv, per * k:per * (k + 1)].rearrange("l d e -> d l e"),
                             slot(u, per, DK))
            for n, (nn, k) in enumerate(pair_order()):
                u = FIRST[C_OUT] + n
                load(u, w_out[:, UNIT_KT * k:UNIT_KT * (k + 1), nn * NW:(nn + 1) * NW], slot(u))
            for n in (2, 3):
                for k in range(UPC):
                    u = FIRST[C_OUT + n] + k
                    load(u, w_out[:, UNIT_KT * k:UNIT_KT * (k + 1), n * NW:(n + 1) * NW], slot(u))
            w1, w2 = rows(mlp_w1), rows(mlp_w2)
            with sp.Fori(0, QUARTERS) as q:
                with sp.Fori(0, 4) as j:
                    for k in range(UPC):
                        u = FIRST[C_MLP] + k
                        load(u, w1[:, UNIT_KT * k:UNIT_KT * (k + 1), bass.ds(q * D + j * NW, NW)],
                             slot(u), q * (8 * UPC) + j * UPC)
                with sp.Fori(0, 4) as j:
                    for k in range(UPC):
                        u = FIRST[C_MLP + 4] + k
                        load(u, w2[:, bass.ds(q * KT + UNIT_KT * k, UNIT_KT), bass.ds(j * NW, NW)],
                             slot(u), q * (8 * UPC) + j * UPC)
            w_gate, w_proj = rows(ple_w_gate), rows(ple_w_proj)
            for n in range(4):
                u = FIRST[C_PLE + n]
                load(u, w_proj[:, :, n * NW:(n + 1) * NW], slot(u))
                for k in range(UPC):
                    load(u + 1 + k, w_gate[:, UNIT_KT * k:UNIT_KT * (k + 1), n * NW:(n + 1) * NW],
                         slot(u + 1 + k))
            out_v = out[0].rearrange("(t p) d -> p t d", p=P)
            for n in range(4):
                for t in range(TT):
                    sp.wait_ge(out_ready, TT * n + t + 1)
                    sp.dma_start(out_v[:, t, n * NW:(n + 1) * NW],
                                 h[:, t, n * NW:(n + 1) * NW]).then_inc(out_stored, 16)
            sp.wait_ge(out_stored, 16 * 4 * TT)

        @block.gpsimd
        def _(pool):
            nc.gpsimd.memset(ident[:], 0.0)
            nc.gpsimd.memset(causal[:], 0.0)
            nc.gpsimd.memset(cmp_neg[:], 0.0)
            nc.gpsimd.memset(cmp_one[:], 1.0)
            nc.gpsimd.memset(minus_half[:], -0.5).then_inc(set_up, 1)
            pool.wait_ge(set_up, 1)
            nc.gpsimd.affine_select(out=ident[:], in_=ident[:], compare_op=ALU.not_equal, fill=1.0, base=0,
                                    pattern=[[-1, P]], channel_multiplier=1).then_inc(set_up, 1)
            nc.gpsimd.affine_select(out=causal[:, P:], in_=causal[:, P:], compare_op=ALU.is_ge, fill=NEG,
                                    base=0, pattern=[[-1, P]], channel_multiplier=1)
            for m, fill in ((cmp_neg, NEG), (cmp_one, 0.0)):
                last = nc.gpsimd.affine_select(out=m[:], in_=m[:], compare_op=ALU.is_ge, fill=fill,
                                               base=1 - CL, pattern=[[P, TT], [-16, N_CMP]],
                                               channel_multiplier=1)
            last.then_inc(set_up, 1)

            def power(n, rows, cols, dst=None):
                pool.wait_ge(ms_ready, n + 1)
                o = rs8[0:rows, 0:cols] if dst is None else dst
                nc.gpsimd.tensor_tensor(o, ms[0:rows, 0:cols], minus_half[0:rows, 0:cols],
                                        ALU.pow).then_inc(rs_ready, 1)

            power(0, P, TT, rstd[:, 0])
            power(1, P, 8)
            power(2, P, 8)
            power(3, N_CMP, G)
            for g in range(G):
                power(4 + g, P, 8)
            power(8, P, TT, rstd[:, 1])

            def square(c, i=0):
                for t in range(TT):
                    pool.wait_ge(acc_read[c % 2][t], c // 2 + 1 + 4 * i)
                    nc.gpsimd.tensor_tensor(stage[:, t], stage[:, t], stage[:, t], ALU.mult)\
                      .then_inc(squared, 1)

            with pool.Fori(0, QUARTERS) as q:
                for j in range(4):
                    square(C_MLP + j, q)
            power(9, P, TT, rstd[:, 2])

        @block.scalar
        def _(act):
            act.dma_start(const_rows[GAIN_MIX:GAIN_MIX + KT], norm_mix_g[0].rearrange("(t p) -> t p", p=P)).then_inc(const_full, 16)
            act.dma_start(const_rows[GAIN_MLP:GAIN_MLP + KT], norm_mlp_g[0].rearrange("(t p) -> t p", p=P)).then_inc(const_full, 16)
            act.dma_start(const_rows[GAIN_PLE:GAIN_PLE + KT], ple_norm_g[0].rearrange("(t p) -> t p", p=P)).then_inc(const_full, 16)
            act.dma_start(const_rows[GAIN_Q:GAIN_Q + 1], nsa_q_g).then_inc(const_full, 16)
            act.dma_start(const_rows[GAIN_K:GAIN_K + 3], nsa_k_g[0]).then_inc(const_full, 16)
            act.dma_start(const_rows[POS:POS + 2 * CL], nsa_cmp_pos[0].rearrange("k l d -> (k l) d")).then_inc(const_full, 16)
            act.dma_start(cmp_w2[:], nsa_cmp_w2[0].rearrange("k d e -> d k e")).then_inc(cmp_w2_full, 16)
            act.dma_start(p_rows[:], p[0, 0].rearrange("(t p) d -> p t d", p=P)).then_inc(p_full, 16)
            steps = [0]

            def link(ins):
                steps[0] += 1
                ins.then_inc(act_step, 1)
                act.wait_ge(act_step, steps[0])

            def split_hi(first, n, i=0, width=UW):
                for k in range(n):
                    u = first + k
                    act.wait_ge(raw_full[u % RAW], 16 * (u // RAW + 1) + 16 * UPC * i)
                    if not (isinstance(i, int) and u < SPLIT):
                        act.wait_ge(unit_used, u - SPLIT + 1 + 8 * UPC * i)
                    nc.scalar.activation(w_hi[:, u % SPLIT, 0:width], w_raw[:, u % RAW, 0:width],
                                         ACT.Copy).then_inc(hi_done, 1)
                    yield k

            def evac(c, dst, func=ACT.Copy, scale=1.0, i=0):
                act.wait_ge(unit_used, END[c] + 8 * UPC * i)
                for t in range(TT):
                    nc.scalar.activation(dst(t), acc[c % 2][t][:, 0:GATES] if c == C_GATE else acc[c % 2][t][:],
                                         func, scale=scale[:, t:t + 1]).then_inc(acc_read[c % 2][t], 1)

            def transposed_hi(r, dst_hi, kt0, gain, i=0):
                for b in range(2):
                    act.wait_ge(tr_full[b], r + 1 + 4 * i)
                    if gain is None:
                        last = nc.scalar.activation(
                            dst_hi[:, kt0 + 2 * b:kt0 + 2 * b + 2].rearrange("p k s -> p (k s)"), tr[b][:], ACT.Copy)
                    else:
                        for m in range(2):
                            kt = kt0 + 2 * b + m
                            last = nc.scalar.activation(dst_hi[:, kt], tr[b][:, m * SEQ:(m + 1) * SEQ], ACT.Copy,
                                                        scale=const_t[:, gain + kt:gain + kt + 1])
                    last.then_inc(tr_hi[b], 1)

            def sum_squares(norm, n):
                for t in range(TT):
                    ins = nc.scalar.activation(junk_act[:], h[:, t, n * NW:(n + 1) * NW], ACT.Square,
                                               accum_out=ss[:, norm, t, n:n + 1])
                    if n == 3 and t == TT - 1:
                        ins.then_inc(sums_ready, 1)
                        act.wait_ge(sums_ready, norm + 1)
                    else:
                        link(ins)

            def h_chunk_stats(c, norm, n):
                for t in range(TT):
                    act.wait_ge(acc_read[c % 2][t], c // 2 + 1)
                sum_squares(norm, n)

            def pos_part(kv):
                for half in range(2):
                    if half:
                        for b in range(2):
                            act.wait_ge(tr_done[b], R_KC + kv + 1)
                    else:
                        act.wait_ge(pos_added, kv + 1)
                    nc.scalar.activation(b_hi[:, 8 * kv + 4 * half:8 * kv + 4 * half + 4].rearrange("p k s -> p (k s)"),
                                         junk[:], ACT.Copy).then_inc(pos_hi, 1)

            def hidden(kv):
                act.wait_ge(unit_used, CMP_FIRST[kv] + CMP_UNITS)
                if kv:
                    act.wait_ge(hid_ready, kv)
                nc.scalar.activation(hid_e[:], sc[0][:, 0:4 * N_CMP], ACT.Exp, scale=-1.0).then_inc(hid_exp, 1)

            def head_exp(hh):
                par = hh % 2
                act.wait_ge(s_read, hh + 1)
                for t in range(TT):
                    for br in range(2):
                        s = (s1 if t else s0)[:, par, br]
                        last = nc.scalar.activation(s, s, ACT.Exp, bias=nmx[:, par, 2 * t + br:2 * t + br + 1],
                                                    scale=SCALE, accum_out=sm[:, par, 2 * t + br:2 * t + br + 1])
                last.then_inc(s_exp, 1)

            def head_pt(hh):
                act.wait_ge(tr_full[0], p_set(hh) + 1)
                if hh >= 2:
                    act.wait_ge(o_full, hh - 1)
                nc.scalar.activation(p_t[:, hh % 2, 0:NW], tr[0][:], ACT.Copy).then_inc(tr_done[0], 1)

            def head_o(hh):
                act.wait_ge(o_full, hh + 1)
                nc.scalar.activation(b_hi[:, hh], sc[0][:, 0:SEQ], ACT.Copy).then_inc(o_hi, 1)

            def cmp_softmax(g):
                act.wait_ge(cmp_read, g + 1)
                nc.scalar.activation(cmp_s[:], cmp_s[:], ACT.Exp, scale=SCALE).then_inc(cmp_exp, 1)

            def to_stage(c, scale):
                evac(c, lambda t: stage[:, t], scale=scale)

            act.wait_ge(consts_ready, 1)
            transposed_hi(R_X, a_hi, 0, GAIN_MIX)
            for k in split_hi(FIRST[C_KC], UPC):
                if k in (1, 3, 5):
                    n = (k + 1) // 2
                    transposed_hi(R_X + n, a_hi, 4 * n, GAIN_MIX)
                if k == 6:
                    for n in range(4):
                        act.wait_ge(x_full[n], 16)
                        sum_squares(0, n)
            for k in split_hi(FIRST[C_VC], UPC):
                if k == 2:
                    act.wait_ge(rs_ready, 1)
                    to_stage(C_KC, rstd[:, 0])
                if k == 6:
                    pos_part(0)
            for k in split_hi(FIRST[C_KS], UPC):
                if k == 2:
                    act.wait_ge(tr_full[1], R_KC + 1)
                    to_stage(C_VC, rstd[:, 0])
                if k == 6:
                    pos_part(1)
            for k in split_hi(CMP_FIRST[0], CMP_UNITS):
                pass
            for k in split_hi(FIRST[C_KW], UPC):
                if k == 0:
                    act.wait_ge(tr_full[1], R_VC + 1)
                    to_stage(C_KS, rstd[:, 0])
                if k == 3:
                    hidden(0)
            for k in split_hi(CMP_FIRST[1], CMP_UNITS):
                pass
            for k in split_hi(FIRST[C_VS], UPC):
                if k == 0:
                    act.wait_ge(tr_full[1], R_KS + 1)
                    to_stage(C_KW, rstd[:, 0])
                if k == 1:
                    act.wait_ge(kc_full, 1)
                    nc.scalar.activation(kc_rows[:], sc[1][0:N_CMP, :], ACT.Copy).then_inc(kc_copied, 1)
                if k == 3:
                    hidden(1)
            for k in split_hi(FIRST[C_VW], UPC):
                if k == 2:
                    evac(C_VS, lambda t: v_slc[:, t], scale=rstd[:, 0])
                if k == 3:
                    act.wait_ge(vc_full, 1)
                    nc.scalar.activation(v_cmp[:], sc[0][0:N_CMP, :], ACT.Copy).then_inc(vc_ready, 1)
                if k == 6:
                    for b in range(2):
                        act.wait_ge(tr_full[b], R_P + 1)
                        nc.scalar.activation(pt_hi[:, b], tr[b][:, 0:SEQ], ACT.Copy).then_inc(tr_hi[b], 1)
            for k in split_hi(FIRST[C_GATE], 1, width=KT * GATES):
                pass
            for k in split_hi(FIRST[C_Q], UPC):
                if k == 1:
                    evac(C_VW, lambda t: v_win[:, t], scale=rstd[:, 0])
                if k == 2:
                    act.wait_ge(neg_ready, 1)
                    evac(C_GATE, lambda t: gates[:, t], ACT.Exp, neg_rstd)
            for g in range(G + 1):
                first = FIRST[C_Q + g + 1] if g < G else FIRST[C_OUT] + UPC
                for k in split_hi(first, UPC):
                    n = HPG * (g - 1)
                    if k == 0:
                        if g >= 2:
                            head_o(n - 1)
                        if g:
                            head_exp(n + 1)
                    if k == 1 and g:
                        head_pt(n)
                    if k == 2:
                        if g < G:
                            act.wait_ge(tr_full[1], q_set(g - 1) + 1 if g else R_KW + 1)
                            to_stage(C_Q + g, rstd[:, 0])
                        if g:
                            head_o(n)
                    if k == 3 and g:
                        head_exp(n + 2)
                        head_pt(n + 1)
                    if k == 4 and g:
                        head_o(n + 1)
                    if k == 5 and g:
                        head_exp(n + 3)
                        head_pt(n + 2)
                    if k == 6:
                        if g:
                            head_o(n + 2)
                        if g < G:
                            cmp_softmax(g)
                    if k == 7:
                        if g < G:
                            head_exp(n + 4)
                        if g:
                            head_pt(n + 3)
                        if g == G:
                            head_o(n + 3)
            for k in split_hi(FIRST[C_OUT + 2], UPC):
                if k in (1, 2):
                    h_chunk_stats(C_OUT + k - 1, 1, k - 1)
                if k in (4, 6):
                    n = k // 2 - 2
                    transposed_hi(R_H1 + n, a_hi, 4 * n, GAIN_MLP)
            for k in split_hi(FIRST[C_OUT + 3], UPC):
                if k == 2:
                    h_chunk_stats(C_OUT + 2, 1, 2)
                if k == 4:
                    transposed_hi(R_H1 + 2, a_hi, 8, GAIN_MLP)
            for k in split_hi(FIRST[C_MLP], UPC):
                if k == 2:
                    h_chunk_stats(C_OUT + 3, 1, 3)
                if k == 4:
                    transposed_hi(R_H1 + 3, a_hi, 12, GAIN_MLP)
            act.wait_ge(rs_ready, 9)

            def hidden_chunks(chunks, i):
                for j in chunks:
                    for k in split_hi(FIRST[C_MLP + j], UPC, i):
                        if k == 2:
                            evac(C_MLP + j - 1, lambda t: stage[:, t], ACT.Relu, rstd[:, 1], i)
                        if k == 4:
                            transposed_hi(R_MLP + j - 1, b_hi, 4 * (j - 1), None, i)

            with act.Fori(0, QUARTERS - 1) as q:
                hidden_chunks(range(1, 5), q)
                for j in range(5, 9):
                    for k in split_hi(FIRST[C_MLP + j], UPC, q):
                        pass
            last_q = QUARTERS - 1
            hidden_chunks(range(1, 5), last_q)
            for n in range(4):
                c = C_MLP + 8 * last_q + 4 + n
                first = FIRST[c + 1]
                for k in split_hi(first, UPC + 1 if n == 3 else UPC):
                    if k == 2:
                        h_chunk_stats(c, 2, n)
                    if k == 4:
                        transposed_hi(R_H2 + n, a_hi, 4 * n, GAIN_PLE)
            act.wait_ge(rs_ready, 10)
            for n in range(4):
                def gate_out(n):
                    act.wait_ge(unit_used, END[C_PLE + n])
                    c = C_PLE + n
                    if n:
                        act.wait_ge(out_ready, TT * n)
                    for t in range(TT):
                        nc.scalar.activation(stage[:, t], acc[c % 2][t][:], ACT.Sigmoid,
                                             scale=rstd[:, 2, t:t + 1]).then_inc(acc_read[c % 2][t], 1)
                if n < 3:
                    for k in split_hi(FIRST[C_PLE + n + 1], UPC + 1):
                        if k == 2:
                            gate_out(n)
                else:
                    gate_out(n)

        @block.vector
        def _(dve):
            steps = [0]

            def link(ins):
                steps[0] += 1
                ins.then_inc(dve_step, 1)
                dve.wait_ge(dve_step, steps[0])

            def split_lo(first, n, i=0, width=UW):
                for k in range(n):
                    u = first + k
                    dve.wait_ge(hi_done, u + 1 + 8 * UPC * i)
                    nc.vector.tensor_tensor(w_lo[:, u % SPLIT, 0:width], w_raw[:, u % RAW, 0:width],
                                            f32(w_hi[:, u % SPLIT, 0:width]), ALU.subtract).then_inc(lo_done, 1)
                    yield k

            def transposed_lo(r, hi, lo, kt0, gain, i=0):
                for b in range(2):
                    dve.wait_ge(tr_hi[b], hi_sets(r) + 4 * i)
                    if gain is None:
                        last = nc.vector.tensor_tensor(
                            flat(lo, kt0 + 2 * b, 2), tr[b][:], f32(flat(hi, kt0 + 2 * b, 2)), ALU.subtract)
                    else:
                        for m in range(2):
                            kt = kt0 + 2 * b + m
                            last = nc.vector.scalar_tensor_tensor(
                                out=lo[:, kt], in0=tr[b][:, m * SEQ:(m + 1) * SEQ],
                                scalar=const_t[:, gain + kt:gain + kt + 1], in1=f32(hi[:, kt]),
                                op0=ALU.mult, op1=ALU.subtract)
                    last.then_inc(tr_done[b], 1)

            def mean_square(n, norm):
                dve.wait_ge(sums_ready, norm + 1)
                link(nc.vector.reduce_sum(head_sums[:, 0:TT], ss[:, norm], axis=AXX))
                if n:
                    dve.wait_ge(rs_ready, n)
                nc.vector.tensor_scalar(ms[:, 0:TT], head_sums[:, 0:TT], 1.0 / D, EPS, ALU.mult,
                                        ALU.add).then_inc(ms_ready, 1)

            def heads_mean_square(n, src, squares, rows, cols):
                link(nc.vector.tensor_tensor(squares, src, src, ALU.mult))
                link(nc.vector.reduce_sum(head_sums[0:rows, 0:cols], squares, axis=AXX))
                dve.wait_ge(rs_ready, n)
                nc.vector.tensor_scalar(ms[0:rows, 0:cols], head_sums[0:rows, 0:cols], 1.0 / DK, EPS,
                                        ALU.mult, ALU.add).then_inc(ms_ready, 1)

            def heads_scale(n, src, rows, cols, done):
                dve.wait_ge(rs_ready, n + 1)
                nc.vector.tensor_tensor(src, src, rs8[0:rows, 0:cols, None].to_broadcast([rows, cols, DK]),
                                        ALU.mult).then_inc(done, 1)

            stage_v = stage[:].rearrange("p t (a d) -> p (t a) d", d=DK)
            junk_v = junk[:].rearrange("p (a d) -> p a d", d=DK)
            kc_v = kc_rows[:].rearrange("p (a d) -> p a d", d=DK)
            kc_sq_v = kc_sq[:].rearrange("p (a d) -> p a d", d=DK)

            def staged_mean_square(n, c):
                for t in range(TT):
                    dve.wait_ge(acc_read[c % 2][t], c // 2 + 1)
                heads_mean_square(n, stage_v, junk_v, P, TT * HPG)

            def staged_scale(n):
                heads_scale(n, stage_v, P, TT * HPG, normed)

            def keys_out(r, br):
                for b in range(2):
                    dve.wait_ge(tr_full[b], r + 1)
                    nc.vector.tensor_scalar(k_t[:, 2 * b:2 * b + 2, :, br],
                                            tr[b][:].rearrange("p (g t s) -> p g t s", g=2, t=TT),
                                            const_t[:, GAIN_K + 1 + br:GAIN_K + 2 + br], None, ALU.mult)\
                      .then_inc(tr_done[b], 1)

            def queries_out(g):
                for b in range(2):
                    dve.wait_ge(tr_full[b], q_set(g) + 1)
                    nc.vector.tensor_scalar(q_t[:, 2 * b:2 * b + 2], tr[b][:].rearrange("p (m s) -> p m s", m=2),
                                            const_t[:, GAIN_Q:GAIN_Q + 1], None, ALU.mult).then_inc(tr_done[b], 1)

            def pos_part(kv):
                r = R_KC + kv
                for half in range(2):
                    for b in range(2):
                        if not half:
                            dve.wait_ge(tr_full[b], r + 1)
                        col = POS + kv * CL + half * (CL // 2)
                        ins = nc.vector.tensor_tensor(
                            junk[:, b * NW:(b + 1) * NW].rearrange("p (m l) -> p m l", l=CL // 2),
                            tr[b][:].rearrange("p (m l) -> p m l", l=CL // 2),
                            const_t[:, None, col:col + CL // 2].to_broadcast([P, NW // (CL // 2), CL // 2]), ALU.add)
                        if half:
                            ins.then_inc(tr_done[b], 1)
                        elif b:
                            ins.then_inc(pos_added, 1)
                    dve.wait_ge(pos_hi, 2 * kv + half + 1)
                    kt0 = 8 * kv + 4 * half
                    ins = nc.vector.tensor_tensor(flat(b_lo, kt0, 4), junk[:], f32(flat(b_hi, kt0, 4)), ALU.subtract)
                    ins.then_inc(pos_split, 1)
                    dve.wait_ge(pos_split, 2 * kv + half + 1)

            def hidden(kv):
                dve.wait_ge(hid_exp, kv + 1)
                if kv:
                    dve.wait_ge(kc_full, 1)
                link(nc.vector.tensor_scalar(hid_e[:], hid_e[:], 1.0, None, ALU.add))
                link(nc.vector.reciprocal(hid_e[:], hid_e[:]))
                nc.vector.tensor_tensor(hid[:], sc[0][:, 0:4 * N_CMP], hid_e[:], ALU.mult).then_inc(hid_ready, 1)

            def head_max(hh):
                par = hh % 2
                dve.wait_ge(s_full, hh + 1)
                for t in range(TT):
                    for br in range(2):
                        if t:
                            scores = sc[1][:].rearrange("p (t b s) -> p t b s", t=TT, b=2)[:, :, br]
                            masked = s1[:, par, br].rearrange("p (t s) -> p t s", t=TT)
                            mask = causal[:].rearrange("p (t s) -> p t s", t=TT)
                        else:
                            scores, masked, mask = sc[0][:, br * P:(br + 1) * P], s0[:, par, br], causal[:, P:]
                        m = 2 * t + br
                        ins = nc.vector.tensor_tensor_reduce(out=masked, in0=scores, in1=mask, scale=1.0,
                                                             scalar=-3e38, op0=ALU.add, op1=ALU.max,
                                                             accum_out=mx[:, par, m:m + 1])
                link(ins)
                nc.vector.tensor_scalar(nmx[:, par], mx[:, par], -SCALE, None, ALU.mult).then_inc(s_read, 1)

            def head_scale(hh):
                par = hh % 2
                dve.wait_ge(s_exp, hh + 1)
                link(nc.vector.tensor_scalar(sm[:, par], sm[:, par], 1e-30, None, ALU.max))
                link(nc.vector.reciprocal(cf[:, par], sm[:, par]))
                c4 = cf[:, par].rearrange("p (t b) -> p t b", t=TT)
                link(nc.vector.tensor_tensor(c4, c4, gates[:, :, 3 * hh + 1:3 * hh + 3], ALU.mult))
                for t in range(TT):
                    for br in range(2):
                        s = (s1 if t else s0)[:, par, br]
                        ins = nc.vector.tensor_scalar(s, s, cf[:, par, 2 * t + br:2 * t + br + 1], None, ALU.mult)
                ins.then_inc(s_scaled, 1)

            def cmp_max(g):
                dve.wait_ge(cmp_full, g + 1)
                scores = sc[1][:, 0:TT * HPG * N_CMP].rearrange("p (t j n) -> p t j n", t=TT, j=HPG)
                link(nc.vector.tensor_tensor(cmp_s[:], scores,
                                             cmp_neg[:, :, None, :].to_broadcast([P, TT, HPG, N_CMP]), ALU.add))
                rows = cmp_s[:].rearrange("p t j n -> p (t j) n")
                link(nc.vector.reduce_max(cmp_m[:], rows, axis=AXX))
                nc.vector.tensor_tensor(rows, rows, cmp_m[:, :, None].to_broadcast([P, TT * HPG, N_CMP]),
                                        ALU.subtract).then_inc(cmp_read, 1)

            def cmp_scale(g):
                dve.wait_ge(cmp_exp, g + 1)
                link(nc.vector.tensor_tensor(cmp_s[:], cmp_s[:],
                                             cmp_one[:, :, None, :].to_broadcast([P, TT, HPG, N_CMP]), ALU.mult))
                rows = cmp_s[:].rearrange("p t j n -> p (t j) n")
                link(nc.vector.reduce_sum(cmp_c[:], rows, axis=AXX))
                link(nc.vector.tensor_scalar(cmp_c[:], cmp_c[:], 1e-30, None, ALU.max))
                link(nc.vector.reciprocal(cmp_c[:], cmp_c[:]))
                c8 = cmp_c[:].rearrange("p (t j) -> p t j", t=TT)
                own = gates[:, :, 3 * HPG * g:3 * HPG * (g + 1)].rearrange("p t (j b) -> p t j b", b=3)[:, :, :, 0]
                link(nc.vector.tensor_tensor(c8, c8, own, ALU.mult))
                nc.vector.tensor_tensor(cmp_p[:, g % 2].rearrange("p t j n -> p (t j) n"), rows,
                                        cmp_c[:, :, None].to_broadcast([P, TT * HPG, N_CMP]),
                                        ALU.mult).then_inc(cmp_ready, 1)

            def head_pt(hh):
                dve.wait_ge(tr_full[1], p_set(hh) + 1)
                if hh >= 2:
                    dve.wait_ge(o_full, hh - 1)
                nc.vector.tensor_copy(p_t[:, hh % 2, NW:NW + SEQ], tr[1][:, 0:SEQ])
                nc.vector.tensor_copy(p_t[0:N_CMP, hh % 2, NW + SEQ:2 * NW], tr[1][0:N_CMP, SEQ:NW])\
                  .then_inc(tr_done[1], 1)

            def head_o(hh):
                dve.wait_ge(o_hi, hh + 1)
                nc.vector.tensor_tensor(b_lo[:, hh], sc[0][:, 0:SEQ], f32(b_hi[:, hh]), ALU.subtract)\
                  .then_inc(o_done, 1)

            def add_to_h(c, n, i=0):
                dve.wait_ge(unit_used, END[c] + 8 * UPC * i)
                for t in range(TT):
                    cols = h[:, t, n * NW:(n + 1) * NW]
                    nc.vector.tensor_tensor(cols, acc[c % 2][t][:], cols, ALU.add).then_inc(acc_read[c % 2][t], 1)

            dve.wait_ge(consts_in_psum, 1)
            nc.vector.tensor_copy(const_t[:], sc[0][:, 0:N_CONST]).then_inc(consts_ready, 1)
            dve.wait_ge(consts_ready, 1)
            dve.wait_ge(set_up, 3)
            transposed_lo(R_X, a_hi, a_lo, 0, GAIN_MIX)
            for k in split_lo(FIRST[C_KC], UPC):
                if k in (1, 3, 5):
                    n = (k + 1) // 2
                    transposed_lo(R_X + n, a_hi, a_lo, 4 * n, GAIN_MIX)
            for k in split_lo(FIRST[C_VC], UPC):
                if k == 0:
                    mean_square(0, 0)
                if k == 1:
                    dve.wait_ge(rs_ready, 1)
                    nc.vector.tensor_scalar(neg_rstd[:], rstd[:, 0], -1.0, None, ALU.mult).then_inc(neg_ready, 1)
                if k == 6:
                    pos_part(0)
            for k in split_lo(FIRST[C_KS], UPC):
                if k == 6:
                    pos_part(1)
            for k in split_lo(CMP_FIRST[0], CMP_UNITS):
                pass
            for k in split_lo(FIRST[C_KW], UPC):
                if k == 0:
                    staged_mean_square(1, C_KS)
                if k == 1:
                    staged_scale(1)
                if k == 3:
                    hidden(0)
                if k == 6:
                    keys_out(R_KS, 0)
            for k in split_lo(CMP_FIRST[1], CMP_UNITS):
                pass
            for k in split_lo(FIRST[C_VS], UPC):
                if k == 0:
                    staged_mean_square(2, C_KW)
                if k == 1:
                    staged_scale(2)
                if k == 2:
                    dve.wait_ge(kc_copied, 1)
                    heads_mean_square(3, kc_v, kc_sq_v, N_CMP, G)
                if k == 3:
                    heads_scale(3, kc_v, N_CMP, G, kc_normed)
                    hidden(1)
                if k == 6:
                    keys_out(R_KW, 1)
            for k in split_lo(FIRST[C_VW], UPC):
                if k == 1:
                    dve.wait_ge(kct_full, 1)
                    nc.vector.tensor_scalar(kc_t[:].rearrange("p g n -> p (g n)"), sc[1][:, 0:G * N_CMP],
                                            const_t[:, GAIN_K:GAIN_K + 1], None, ALU.mult).then_inc(kct_ready, 1)
                if k == 6:
                    for b in range(2):
                        dve.wait_ge(tr_hi[b], hi_sets(R_P))
                        nc.vector.tensor_tensor(pt_lo[:, b], tr[b][:, 0:SEQ], f32(pt_hi[:, b]), ALU.subtract)\
                          .then_inc(tr_done[b], 1)
            for k in split_lo(FIRST[C_GATE], 1, width=KT * GATES):
                pass
            for k in split_lo(FIRST[C_Q], UPC):
                if k == 3:
                    for t in range(TT):
                        dve.wait_ge(acc_read[C_GATE % 2][t], C_GATE // 2 + 1)
                    link(nc.vector.tensor_scalar(gates[:], gates[:], 1.0, None, ALU.add))
                    link(nc.vector.reciprocal(gates[:], gates[:]))
            for g in range(G + 1):
                first = FIRST[C_Q + g + 1] if g < G else FIRST[C_OUT] + UPC
                for k in split_lo(first, UPC):
                    n = HPG * (g - 1)
                    if k == 0:
                        if g >= 2:
                            head_o(n - 1)
                        if g:
                            head_max(n + 1)
                    if k == 1 and g:
                        head_pt(n)
                        head_scale(n + 1)
                    if k == 2:
                        if g < G:
                            staged_mean_square(4 + g, C_Q + g)
                        if g:
                            head_o(n)
                            head_max(n + 2)
                    if k == 3:
                        if g < G:
                            staged_scale(4 + g)
                        if g:
                            head_pt(n + 1)
                            head_scale(n + 2)
                    if k == 4 and g:
                        head_o(n + 1)
                        head_max(n + 3)
                    if k == 5:
                        if g:
                            head_pt(n + 2)
                        if g < G:
                            queries_out(g)
                        if g:
                            head_scale(n + 3)
                    if k == 6:
                        if g:
                            head_o(n + 2)
                        if g < G:
                            cmp_max(g)
                            head_max(n + 4)
                    if k == 7:
                        if g:
                            head_pt(n + 3)
                        if g < G:
                            cmp_scale(g)
                            head_scale(n + 4)
                        if g == G:
                            head_o(n + 3)
            for n in range(4):
                dve.wait_ge(x_full[n], 16)
            for k in split_lo(FIRST[C_OUT + 2], UPC):
                if k in (1, 2):
                    add_to_h(C_OUT + k - 1, k - 1)
                if k in (4, 6):
                    n = k // 2 - 2
                    transposed_lo(R_H1 + n, a_hi, a_lo, 4 * n, GAIN_MLP)
            for k in split_lo(FIRST[C_OUT + 3], UPC):
                if k == 2:
                    add_to_h(C_OUT + 2, 2)
                if k == 4:
                    transposed_lo(R_H1 + 2, a_hi, a_lo, 8, GAIN_MLP)
            for k in split_lo(FIRST[C_MLP], UPC):
                if k == 2:
                    add_to_h(C_OUT + 3, 3)
                if k == 3:
                    mean_square(8, 1)
                if k == 4:
                    transposed_lo(R_H1 + 3, a_hi, a_lo, 12, GAIN_MLP)

            def hidden_chunks(i):
                for j in range(1, 5):
                    for k in split_lo(FIRST[C_MLP + j], UPC, i):
                        if k == 4:
                            transposed_lo(R_MLP + j - 1, b_hi, b_lo, 4 * (j - 1), None, i)

            with dve.Fori(0, QUARTERS - 1) as q:
                hidden_chunks(q)
                for j in range(5, 9):
                    for k in split_lo(FIRST[C_MLP + j], UPC, q):
                        if k == 2:
                            add_to_h(C_MLP + j - 1, j - 5, q)
            last_q = QUARTERS - 1
            hidden_chunks(last_q)
            for n in range(4):
                c = C_MLP + 8 * last_q + 4 + n
                for k in split_lo(FIRST[c + 1], UPC + 1 if n == 3 else UPC):
                    if k == 2:
                        add_to_h(c, n)
                    if k == 3 and n == 3:
                        mean_square(9, 2)
                    if k == 4:
                        transposed_lo(R_H2 + n, a_hi, a_lo, 4 * n, GAIN_PLE)

            def gated_out(n):
                c = C_PLE + n
                for t in range(TT):
                    dve.wait_ge(acc_read[c % 2][t], c // 2 + 1)
                    link(nc.vector.tensor_tensor(stage[:, t], (tr if n % 2 else sc)[t][:], stage[:, t], ALU.mult))
                    cols = h[:, t, n * NW:(n + 1) * NW]
                    nc.vector.tensor_tensor(cols, stage[:, t], cols, ALU.add).then_inc(out_ready, 1)

            for n in range(3):
                for k in split_lo(FIRST[C_PLE + n + 1], UPC + 1):
                    if k == 2:
                        gated_out(n)
            gated_out(3)

        @block.tensor
        def _(pe):
            def bank_free(c, i=0):
                if c >= 2:
                    for t in range(TT):
                        pe.wait_ge(acc_read[c % 2][t], c // 2 + 4 * i)

            def unit(c, u, k, x_hi, x_lo, i=0):
                if k == 0:
                    bank_free(c, i)
                pe.wait_ge(lo_done, u + 1 + 8 * UPC * i)
                for m in range(UNIT_KT):
                    kt = UNIT_KT * k + m
                    for t in range(TT):
                        toks = slice(t * P, (t + 1) * P)
                        for n, (xs, ws) in enumerate(((x_hi, w_hi), (x_hi, w_lo), (x_lo, w_hi))):
                            last = nc.tensor.matmul(acc[c % 2][t][:], xs[:, kt, toks],
                                                    ws[:, u % SPLIT, m * NW:(m + 1) * NW],
                                                    start=(kt == 0 and n == 0), stop=(kt == KT - 1 and n == 2))
                last.then_inc(unit_used, 1)

            def gate_unit(c, u):
                bank_free(c)
                pe.wait_ge(lo_done, u + 1)
                for kt in range(KT):
                    for t in range(TT):
                        toks = slice(t * P, (t + 1) * P)
                        for n, (xs, ws) in enumerate(((a_hi, w_hi), (a_hi, w_lo), (a_lo, w_hi))):
                            last = nc.tensor.matmul(acc[c % 2][t][:, 0:GATES], xs[:, kt, toks],
                                                    ws[:, u % SPLIT, kt * GATES:(kt + 1) * GATES],
                                                    start=(kt == 0 and n == 0), stop=(kt == KT - 1 and n == 2))
                last.then_inc(unit_used, 1)

            def ple_unit(n, u):
                banks = tr if n % 2 else sc
                if n >= 2:
                    pe.wait_ge(out_ready, TT * (n - 1))
                pe.wait_ge(lo_done, u + 1)
                for t in range(TT):
                    for kt in range(PLE // P):
                        toks = slice(t * P, (t + 1) * P)
                        for m, (xs, ws) in enumerate(((pt_hi, w_hi), (pt_hi, w_lo), (pt_lo, w_hi))):
                            last = nc.tensor.matmul(banks[t][:], xs[:, kt, toks],
                                                    ws[:, u % SPLIT, kt * NW:(kt + 1) * NW],
                                                    start=(kt == 0 and m == 0), stop=(kt == 1 and m == 2))
                last.then_inc(unit_used, 1)

            def transpose_set(r, src, i=0):
                for b in range(2):
                    if r:
                        pe.wait_ge(tr_done[b], r + 4 * i)
                    for m in range(2):
                        for t in range(TT):
                            last = nc.tensor.transpose(tr[b][:, m * SEQ + t * P:m * SEQ + (t + 1) * P],
                                                       src(t, 2 * b + m), ident[:])
                    last.then_inc(tr_full[b], 1)

            def from_stage(t, b):
                return stage[:, t, b * P:(b + 1) * P]

            def from_h(n):
                return lambda t, b: h[:, t, n * NW + b * P:n * NW + (b + 1) * P]

            def staged(c):
                for t in range(TT):
                    pe.wait_ge(acc_read[c % 2][t], c // 2 + 1)

            def split_by(r, k, i=0):
                pe.wait_ge(tr_done[k % 2], r + k // 2 + 1 + 4 * i)

            def compress(kv):
                pe.wait_ge(pos_split, 2 * (kv + 1))
                if kv:
                    pe.wait_ge(hid_ready, 1)
                per = CL // CMP_UNITS
                for k in range(CMP_UNITS):
                    u = CMP_FIRST[kv] + k
                    pe.wait_ge(lo_done, u + 1)
                    for m in range(per):
                        pos = per * k + m
                        half, l = divmod(pos, CL // 2)
                        kt0 = 8 * kv + 4 * half
                        hi, lo = (flat(x, kt0, 4).rearrange("p (g n l) -> p n g l", g=G, l=CL // 2)
                                  [:, half:half + N_CMP, :, l] for x in (b_hi, b_lo))
                        wh, wl = (w[:, u % SPLIT, m * DK:(m + 1) * DK] for w in (w_hi, w_lo))
                        for n, (ws, xs) in enumerate(((wh, hi), (wh, lo), (wl, hi))):
                            last = nc.tensor.matmul(sc[0][:, 0:G * N_CMP], ws, xs, start=(pos == 0 and n == 0),
                                                    stop=(pos == CL - 1 and n == 2))
                    last.then_inc(unit_used, 1)

            def second_layer(kv, bank, done):
                pe.wait_ge(hid_ready, kv + 1)
                hid_v = hid[:].rearrange("p (n g) -> p n g", g=G)
                for g in range(G):
                    last = nc.tensor.matmul(bank[0:N_CMP, g * DK:(g + 1) * DK], hid_v[:, :, g],
                                            cmp_w2[:, kv], start=True, stop=True)
                last.then_inc(done, 1)

            def head_scores(hh):
                j, g = hh % HPG, hh // HPG
                if hh:
                    pe.wait_ge(s_read, hh)
                if hh >= 2:
                    pe.wait_ge(o_done, hh - 1)
                pe.wait_ge(cmp_read, g + 1)
                keys = k_t[:, g].rearrange("p t b s -> p (t b s)")
                nc.tensor.matmul(sc[0][:, 0:SEQ], q_t[:, j, 0:P], keys[:, 0:SEQ], start=True, stop=True)
                nc.tensor.matmul(sc[1][:], q_t[:, j, P:SEQ], keys, start=True, stop=True).then_inc(s_full, 1)

            def cmp_scores(g):
                for b in range(2):
                    pe.wait_ge(tr_done[b], q_set(g) + 1)
                if g:
                    pe.wait_ge(s_read, HPG * g)
                else:
                    pe.wait_ge(kct_ready, 1)
                    pe.wait_ge(vc_ready, 1)
                for t in range(TT):
                    for j in range(HPG):
                        at = (t * HPG + j) * N_CMP
                        last = nc.tensor.matmul(sc[1][:, at:at + N_CMP], q_t[:, j, t * P:(t + 1) * P], kc_t[:, g],
                                                start=True, stop=True)
                last.then_inc(cmp_full, 1)

            def head_transpose(hh):
                par, j, g, r = hh % 2, hh % HPG, hh // HPG, p_set(hh)
                pe.wait_ge(s_scaled, hh + 1)
                pe.wait_ge(cmp_ready, g + 1)
                pe.wait_ge(tr_done[0], r)
                for br in range(2):
                    nc.tensor.transpose(tr[0][:, br * SEQ:br * SEQ + P], s0[:, par, br], ident[:])
                    last = nc.tensor.transpose(tr[0][:, br * SEQ + P:(br + 1) * SEQ], s1[:, par, br, 0:P], ident[:])
                last.then_inc(tr_full[0], 1)
                pe.wait_ge(tr_done[1], r)
                for br in range(2):
                    nc.tensor.transpose(tr[1][:, br * P:(br + 1) * P], s1[:, par, br, P:SEQ], ident[:])
                for t in range(TT):
                    last = nc.tensor.transpose(tr[1][0:N_CMP, SEQ + t * P:SEQ + (t + 1) * P],
                                               cmp_p[:, g % 2, t, j], ident[:])
                last.then_inc(tr_full[1], 1)

            def head_output(hh):
                par, g, r = hh % 2, hh // HPG, p_set(hh)
                for b in range(2):
                    pe.wait_ge(tr_done[b], r + 1)
                pe.wait_ge(s_read, min(hh + 2, H))
                cols = slice(g * DK, (g + 1) * DK)
                pt, o = p_t[:, par], sc[0][:, 0:SEQ]
                nc.tensor.matmul(o, v_slc[:, 0, cols], pt[:, 0:SEQ], start=True, stop=False)
                nc.tensor.matmul(o, v_win[:, 0, cols], pt[:, SEQ:2 * SEQ], start=False, stop=False)
                nc.tensor.matmul(o[:, P:SEQ], v_slc[:, 1, cols], pt[:, NW:NW + P], start=False, stop=False)
                nc.tensor.matmul(o[:, P:SEQ], v_win[:, 1, cols], pt[:, NW + P:NW + SEQ], start=False, stop=False)
                nc.tensor.matmul(o, v_cmp[:, cols], pt[0:N_CMP, NW + SEQ:2 * NW], start=False, stop=True)\
                  .then_inc(o_full, 1)

            def attention_step(g, s):
                n = HPG * (g - 1)
                if g:
                    if s in (0, 4):
                        head_scores(n + 2 + s // 4)
                    if s in (1, 5, 9):
                        head_transpose(n + 1 + s // 4)
                    if s in (3, 7, 11):
                        head_output(n + 1 + s // 4)
                if g < G:
                    if s == 6:
                        pe.wait_ge(normed, 3 + g)
                        transpose_set(q_set(g), from_stage)
                    if s == 7:
                        cmp_scores(g)
                    if s in (8, 12):
                        head_scores(n + 4 + (s - 8) // 4)
                    if s == 13:
                        head_transpose(n + 4)
                    if s == 15:
                        head_output(n + 4)

            pe.wait_ge(const_full, 16 * 6)
            pe.wait_ge(set_up, 2)
            nc.tensor.transpose(sc[0][:, 0:N_CONST], const_rows[:], ident[0:N_CONST, 0:N_CONST])\
              .then_inc(consts_in_psum, 1)
            pe.wait_ge(x_full[0], 16)
            transpose_set(R_X, from_h(0))
            for k in range(UPC):
                n = k // 2 + 1
                if k % 2 == 0 and n < 4:
                    pe.wait_ge(x_full[n], 16)
                    transpose_set(R_X + n, from_h(n))
                split_by(R_X, k)
                unit(C_KC, FIRST[C_KC] + k, k, a_hi, a_lo)
            for k in range(UPC):
                if k == 4:
                    staged(C_KC)
                    transpose_set(R_KC, from_stage)
                unit(C_VC, FIRST[C_VC] + k, k, a_hi, a_lo)
            for k in range(UPC):
                if k == 4:
                    staged(C_VC)
                    transpose_set(R_VC, from_stage)
                unit(C_KS, FIRST[C_KS] + k, k, a_hi, a_lo)
            pe.wait_ge(consts_ready, 1)
            compress(0)
            for k in range(UPC):
                if k == 4:
                    pe.wait_ge(normed, 1)
                    transpose_set(R_KS, from_stage)
                if k == 6:
                    pe.wait_ge(cmp_w2_full, 16)
                    second_layer(0, sc[1], kc_full)
                unit(C_KW, FIRST[C_KW] + k, k, a_hi, a_lo)
            compress(1)
            for k in range(UPC):
                if k == 4:
                    pe.wait_ge(normed, 2)
                    transpose_set(R_KW, from_stage)
                if k == 6:
                    second_layer(1, sc[0], vc_full)
                if k == 7:
                    pe.wait_ge(kc_normed, 1)
                    for g in range(G):
                        last = nc.tensor.transpose(sc[1][:, g * N_CMP:(g + 1) * N_CMP],
                                                   kc_rows[:, g * DK:(g + 1) * DK], ident[0:N_CMP, 0:N_CMP])
                    last.then_inc(kct_full, 1)
                unit(C_VS, FIRST[C_VS] + k, k, a_hi, a_lo)
            for k in range(UPC):
                if k == 4:
                    pe.wait_ge(p_full, 16)
                    for b in range(2):
                        pe.wait_ge(tr_done[b], R_P)
                        for t in range(TT):
                            last = nc.tensor.transpose(tr[b][:, t * P:(t + 1) * P],
                                                       p_rows[:, t, b * P:(b + 1) * P], ident[:])
                        last.then_inc(tr_full[b], 1)
                unit(C_VW, FIRST[C_VW] + k, k, a_hi, a_lo)
            gate_unit(C_GATE, FIRST[C_GATE])
            for k in range(UPC):
                unit(C_Q, FIRST[C_Q] + k, k, a_hi, a_lo)
            for g in range(G - 1):
                c = C_Q + g + 1
                for k in range(UPC):
                    for s in (2 * k, 2 * k + 1):
                        attention_step(g, s)
                    unit(c, FIRST[c] + k, k, a_hi, a_lo)
            for n, (nn, k) in enumerate(pair_order()):
                for s in (2 * n, 2 * n + 1):
                    attention_step(G - 1 + s // 16, s % 16)
                pe.wait_ge(o_done, 2 * k + 2)
                unit(C_OUT + nn, FIRST[C_OUT] + n, k, b_hi, b_lo)
            for n in (2, 3):
                c = C_OUT + n
                for k in range(UPC):
                    if k == 2:
                        staged(c - 2 if n == 2 else c - 1)
                        transpose_set(R_H1 + (0 if n == 2 else 2), from_h(0 if n == 2 else 2))
                    if k == 4 and n == 2:
                        staged(c - 1)
                        transpose_set(R_H1 + 1, from_h(1))
                    unit(c, FIRST[c] + k, k, b_hi, b_lo)
            for k in range(UPC):
                if k == 2:
                    staged(C_OUT + 3)
                    transpose_set(R_H1 + 3, from_h(3))
                split_by(R_H1, k)
                unit(C_MLP, FIRST[C_MLP] + k, k, a_hi, a_lo)

            def hidden_chunks(i):
                for j in range(1, 5):
                    for k in range(UPC):
                        if k == 2:
                            pe.wait_ge(squared, TT * j + 4 * TT * i)
                            transpose_set(R_MLP + j - 1, from_stage, i)
                        if j == 4:
                            split_by(R_MLP, k, i)
                        x_hi, x_lo = (b_hi, b_lo) if j == 4 else (a_hi, a_lo)
                        unit(C_MLP + j, FIRST[C_MLP + j] + k, k, x_hi, x_lo, i)

            with pe.Fori(0, QUARTERS - 1) as q:
                hidden_chunks(q)
                for j in range(5, 9):
                    x_hi, x_lo = (b_hi, b_lo) if j < 8 else (a_hi, a_lo)
                    for k in range(UPC):
                        unit(C_MLP + j, FIRST[C_MLP + j] + k, k, x_hi, x_lo, q)
            last_q = QUARTERS - 1
            hidden_chunks(last_q)
            for n in range(3):
                c = C_MLP + 8 * last_q + 5 + n
                for k in range(UPC):
                    if k == 2:
                        staged(c - 1)
                        transpose_set(R_H2 + n, from_h(n))
                    unit(c, FIRST[c] + k, k, b_hi, b_lo)
            for n in range(4):
                c = C_PLE + n
                if n == 1:
                    for b in range(2):
                        pe.wait_ge(tr_done[b], R_H2 + 4)
                ple_unit(n, FIRST[c])
                for k in range(UPC):
                    if n == 0 and k == 2:
                        staged(c - 1)
                        transpose_set(R_H2 + 3, from_h(3))
                    if n == 0:
                        split_by(R_H2, k)
                    unit(c, FIRST[c] + 1 + k, k, a_hi, a_lo)


_INS = ['x', 'p', 'norm_mix_g', 'norm_mlp_g', 'mlp_w1', 'mlp_w2', 'ple_norm_g', 'ple_w_gate', 'ple_w_proj',
        'nsa_w_in', 'nsa_q_g', 'nsa_k_g', 'nsa_cmp_pos', 'nsa_cmp_w1', 'nsa_cmp_w2', 'nsa_w_out']


def kernel(**inputs):
    import numpy as _np
    import concourse.bacc as _bacc
    from concourse import mybir as _mybir
    from concourse.bass_utils import run_bass_kernel_spmd as _run

    nc = _bacc.Bacc("TRN2", target_bir_lowering=False, num_devices=1)
    arrays, args = {}, []
    for name in _INS:
        a = _np.ascontiguousarray(inputs[name])
        arrays[f"in_{name}_dram"] = a
        args.append(nc.dram_tensor(f"in_{name}_dram", a.shape, _mybir.dt.from_np(a.dtype), kind="ExternalInput").ap())
    o = nc.dram_tensor("out_dram", (1, SEQ, D), F32, kind="ExternalOutput").ap()
    trunk_layer(nc, *args, o)
    r = _run(nc, [arrays], core_ids=[0])
    return r.results[0]["out_dram"]
```

```python
from contextlib import ExitStack

import numpy as np

import concourse.bass as bass
from concourse import mybir

F32 = mybir.dt.float32
F32R = mybir.dt.float32r
ACT = mybir.ActivationFunctionType
ALU = mybir.AluOpType
AXX = mybir.AxisListType.X

P = 128
D = 2048
SEQ = 256
TT = SEQ // P
KT = D // P
NW = 512
UNIT_KT = 2
UW = UNIT_KT * NW
UPC = KT // UNIT_KT
RAW = 8
SPLIT = 4
H, G, DK = 16, 4, 128
HPG = H // G
QKV = H * DK
GATES = 3 * H
CSTEP = 16
N_CMP = SEQ // CSTEP - 1
HID = G * (SEQ // CSTEP) - 1
CL = 32
CMP_UNITS = CL * DK // UW
D_FF = 4 * D
QUARTERS = 4
PLE = 256
EPS = 1e-6
NEG = -1e30
SCALE = DK ** -0.5

C_KC, C_VC, C_KS, C_KW, C_VS, C_VW, C_GATE, C_Q = range(8)
C_OUT = C_Q + G
C_MLP = C_OUT + 4
C_PLE = C_MLP + 8 * QUARTERS
W_IN_COL = {C_KC: QKV, C_VC: QKV + NW, C_KS: QKV + 2 * NW, C_VS: QKV + 3 * NW, C_KW: QKV + 4 * NW,
            C_VW: QKV + 5 * NW, C_GATE: QKV + 6 * NW}
W_IN_COL.update({C_Q + g: g * NW for g in range(G)})

FIRST, END, CMP_FIRST = {}, {}, {}


def _number_units():
    u = 0
    for c in range(C_OUT):
        FIRST[c] = u
        u += 1 if c == C_GATE else UPC
        END[c] = u
        if c in (C_KS, C_KW):
            CMP_FIRST[c - C_KS] = u
            u += CMP_UNITS
    FIRST[C_OUT], END[C_OUT], END[C_OUT + 1] = u, u + 2 * UPC - 1, u + 2 * UPC
    u += 2 * UPC
    for c in (C_OUT + 2, C_OUT + 3, *range(C_MLP, C_PLE)):
        FIRST[c], END[c] = u, u + UPC
        u += UPC
    for c in range(C_PLE, C_PLE + 4):
        FIRST[c], END[c] = u, u + 1 + UPC
        u += 1 + UPC


_number_units()


def pair_order():
    first = [(n, k) for n in range(2) for k in range(UPC - 3)]
    return first + [(n, k) for k in range(UPC - 3, UPC) for n in range(2)]


OUT_BLOCKS = [(t, n * NW, NW) for n in range(4) for t in range(TT)][:-1]
OUT_BLOCKS += [(TT - 1, 3 * NW + m * (NW // 2), NW // 2) for m in range(2)]
LATE_UNITS = 4

R_X, R_KC, R_VC, R_KS, R_KW, R_P = 0, 4, 5, 6, 7, 8


def q_set(g):
    return R_P + 5 * g if g else R_P + 1


def p_set(h):
    return R_P + 1 + h + min((h + 1) // HPG + 1, G)


R_H1 = p_set(H - 1) + 1
R_MLP = R_H1 + 4
R_H2 = R_MLP + 4 * QUARTERS


def hi_sets(r):
    return r + 1 if r < R_X + 4 else 5 if r == R_P else r - R_H1 + 6


GAIN_MIX, GAIN_MLP, GAIN_PLE, GAIN_Q, GAIN_K, POS = 0, KT, 2 * KT, 3 * KT, 3 * KT + 1, 3 * KT + 4
N_CONST = POS + 2 * CL


def trunk_layer(nc, x, p, norm_mix_g, norm_mlp_g, mlp_w1, mlp_w2, ple_norm_g, ple_w_gate, ple_w_proj,
                nsa_w_in, nsa_q_g, nsa_k_g, nsa_cmp_pos, nsa_cmp_w1, nsa_cmp_w2, nsa_w_out, out):
    ctx = ExitStack()
    with ctx:
        def sb(name, shape, dt=F32):
            return ctx.enter_context(nc.sbuf_tensor(name, shape, dt))

        def pb(name):
            return ctx.enter_context(nc.psum_tensor(name, [P, NW], F32))

        def sem(name):
            return ctx.enter_context(nc.semaphore(name))

        h = sb("h", [P, TT, D])
        a_hi = sb("a_hi", [P, KT, SEQ], F32R)
        a_lo = sb("a_lo", [P, KT, SEQ], F32R)
        b_hi = sb("b_hi", [P, KT, SEQ], F32R)
        b_lo = sb("b_lo", [P, KT, SEQ], F32R)
        w_raw = sb("w_raw", [P, RAW, UW])
        w_hi = sb("w_hi", [P, SPLIT, UW], F32R)
        w_lo = sb("w_lo", [P, SPLIT, UW], F32R)
        k_t = sb("k_t", [P, G, TT, 2, P])
        v_slc = sb("v_slc", [P, TT, NW])
        v_win = sb("v_win", [P, TT, NW])
        kc_t = sb("kc_t", [P, G, N_CMP])
        v_cmp = sb("v_cmp", [N_CMP, NW])
        kc_rows = sb("kc_rows", [N_CMP, NW])
        kc_sq = sb("kc_sq", [N_CMP, NW])
        q_t = sb("q_t", [P, HPG, SEQ])
        stage = sb("stage", [P, TT, NW])
        junk = sb("junk", [P, 2 * NW])
        junk_act = sb("junk_act", [P, NW])
        gate_rows = junk_act[0:GATES, 0:SEQ]
        s1 = sb("s1", [P, 2, 2, SEQ])
        s0 = sb("s0", [P, 2, 2, P])
        p_t = sb("p_t", [P, 2, 2 * NW])
        mx = sb("mx", [P, 2, 4])
        nmx = sb("nmx", [P, 2, 4])
        sm = sb("sm", [P, 2, 4])
        cf = sb("cf", [P, 2, 4])
        cmp_s = sb("cmp_s", [P, TT, HPG, N_CMP])
        cmp_p = sb("cmp_p", [P, 2, TT, HPG, N_CMP])
        cmp_m = sb("cmp_m", [P, TT * HPG])
        cmp_c = sb("cmp_c", [P, TT * HPG])
        gates = sb("gates", [P, TT, GATES])
        hid_e = sb("hid_e", [HID, DK])
        hid_rows = sb("hid_rows", [HID, DK])
        hid = sb("hid", [P, HID])
        cmp_w2 = sb("cmp_w2", [P, 2, DK])
        ident = sb("ident", [P, P])
        causal = sb("causal", [P, SEQ])
        cmp_neg = sb("cmp_neg", [P, TT, N_CMP])
        cmp_one = sb("cmp_one", [P, TT, N_CMP])
        const_rows = sb("const_rows", [N_CONST, P])
        const_t = sb("const_t", [P, N_CONST])
        ss = sb("ss", [P, 3, TT, 4])
        ms = sb("ms", [P, 8])
        rs8 = sb("rs8", [P, 8])
        minus_half = sb("minus_half", [P, 8])
        rstd = sb("rstd", [P, 3, TT])
        neg_rstd = sb("neg_rstd", [P, TT])
        head_sums = sb("head_sums", [P, 8])
        p_rows = sb("p_rows", [P, TT, PLE])
        pt_hi = sb("pt_hi", [P, 2, SEQ], F32R)
        pt_lo = sb("pt_lo", [P, 2, SEQ], F32R)

        acc = [[pb(f"acc{c}{t}") for t in range(TT)] for c in range(2)]
        sc = [pb("sc0"), pb("sc1")]
        tr = [pb("tr0"), pb("tr1")]

        raw_full = [sem(f"raw_full{n}") for n in range(RAW)]
        x_full = [sem(f"x_full{n}") for n in range(5)]
        mix_full = sem("mix_full")
        const_full = sem("const_full")
        cmp_w2_full = sem("cmp_w2_full")
        p_full = sem("p_full")
        out_stored = sem("out_stored")
        hi_done = sem("hi_done")
        lo_done = sem("lo_done")
        unit_used = sem("unit_used")
        acc_read = [[sem(f"acc_read{c}{t}") for t in range(TT)] for c in range(2)]
        tr_full = [sem(f"tr_full{b}") for b in range(2)]
        tr_hi = [sem(f"tr_hi{b}") for b in range(2)]
        tr_done = [sem(f"tr_done{b}") for b in range(2)]
        set_up = sem("set_up")
        act_step = sem("act_step")
        dve_step = sem("dve_step")
        consts_in_psum = sem("consts_in_psum")
        consts_ready = sem("consts_ready")
        sums_ready = sem("sums_ready")
        ms_ready = sem("ms_ready")
        rs_ready = sem("rs_ready")
        neg_ready = sem("neg_ready")
        normed = sem("normed")
        pos_added = sem("pos_added")
        pos_hi = sem("pos_hi")
        pos_split = sem("pos_split")
        hid_exp = sem("hid_exp")
        hid_ready = sem("hid_ready")
        hid_full = sem("hid_full")
        hid_copied = sem("hid_copied")
        kc_full = sem("kc_full")
        kc_copied = sem("kc_copied")
        kc_normed = sem("kc_normed")
        kct_full = sem("kct_full")
        kct_ready = sem("kct_ready")
        vc_full = sem("vc_full")
        vc_ready = sem("vc_ready")
        gates_full = sem("gates_full")
        gates_exp = sem("gates_exp")
        s_full = sem("s_full")
        s_read = sem("s_read")
        s_exp = sem("s_exp")
        s_scaled = sem("s_scaled")
        cmp_full = sem("cmp_full")
        cmp_read = sem("cmp_read")
        cmp_exp = sem("cmp_exp")
        cmp_ready = sem("cmp_ready")
        o_full = sem("o_full")
        o_hi = sem("o_hi")
        o_done = sem("o_done")
        squared = sem("squared")
        tile_complete = sem("tile_complete")
        out_ready = sem("out_ready")

        block = ctx.enter_context(nc.Block())

        def f32(ap):
            return ap.bitcast(F32)

        def out_bank(hh):
            return sc[0] if hh % HPG == 2 else tr[0]

        def flat(x, kt0, n):
            return x[:, kt0:kt0 + n].rearrange("p k s -> p (k s)")

        @block.sync
        def _(sp):
            def load(u, src, dst, i=0):
                if not (isinstance(i, int) and u < RAW):
                    sp.wait_ge(lo_done, u - RAW + 1 + i)
                sp.dma_start(dst, src).then_inc(raw_full[u % RAW], 16)

            def slot(u, kts=UNIT_KT, n=NW):
                return w_raw[:, u % RAW, 0:kts * n].rearrange("p (k n) -> p k n", n=n)

            def rows(w):
                return w[0].rearrange("(t p) n -> p t n", p=P)

            w_in, w_out = rows(nsa_w_in), rows(nsa_w_out)
            x_v = x[0].rearrange("(t p) d -> p t d", p=P)
            sp.dma_start(const_rows[0:KT], norm_mix_g[0].rearrange("(t p) -> t p", p=P)).then_inc(mix_full, 16)
            for b in range(2):
                cols = slice(b * SEQ, (b + 1) * SEQ)
                sp.dma_start(h[:, :, cols], x_v[:, :, cols]).then_inc(x_full[b], 16)

            def load_const(at, src):
                sp.dma_start(const_rows[at:at + src.shape[0]], src).then_inc(const_full, 16)

            for c in range(C_OUT):
                col = W_IN_COL[c]
                if c == C_GATE:
                    u = FIRST[c]
                    with nc.allow_non_contiguous_dma(reason="gate columns, 192 bytes a row"):
                        load(u, w_in[:, :, col:col + GATES], slot(u, KT, GATES))
                    continue
                for k in range(UPC):
                    u = FIRST[c] + k
                    load(u, w_in[:, UNIT_KT * k:UNIT_KT * (k + 1), col:col + NW], slot(u))
                    if c == 0 and k < 3:
                        n = k + 1
                        sp.dma_start(h[:, :, n * NW:(n + 1) * NW],
                                     x_v[:, :, n * NW:(n + 1) * NW]).then_inc(x_full[n + 1], 16)
                    if c == 0 and k == 5:
                        load_const(GAIN_MLP, norm_mlp_g[0].rearrange("(t p) -> t p", p=P))
                        load_const(GAIN_PLE, ple_norm_g[0].rearrange("(t p) -> t p", p=P))
                        load_const(GAIN_Q, nsa_q_g)
                        load_const(GAIN_K, nsa_k_g[0])
                        load_const(POS, nsa_cmp_pos[0].rearrange("k l d -> (k l) d"))
                    if c == C_VC and k == 3:
                        sp.dma_start(cmp_w2[:], nsa_cmp_w2[0].rearrange("k d e -> d k e")).then_inc(cmp_w2_full, 16)
                        sp.dma_start(p_rows[:], p[0, 0].rearrange("(t p) d -> p t d", p=P)).then_inc(p_full, 16)
                if c in (C_KS, C_KW):
                    kv = c - C_KS
                    per = CL // CMP_UNITS
                    for k in range(CMP_UNITS):
                        u = CMP_FIRST[kv] + k
                        load(u, nsa_cmp_w1[0, kv, per * k:per * (k + 1)].rearrange("l d e -> d l e"),
                             slot(u, per, DK))
            for n, (nn, k) in enumerate(pair_order()):
                u = FIRST[C_OUT] + n
                load(u, w_out[:, UNIT_KT * k:UNIT_KT * (k + 1), nn * NW:(nn + 1) * NW], slot(u))
            for n in (2, 3):
                for k in range(UPC):
                    u = FIRST[C_OUT + n] + k
                    load(u, w_out[:, UNIT_KT * k:UNIT_KT * (k + 1), n * NW:(n + 1) * NW], slot(u))
            w1, w2 = rows(mlp_w1), rows(mlp_w2)
            with sp.Fori(0, QUARTERS) as q:
                with sp.Fori(0, 4) as j:
                    for k in range(UPC):
                        u = FIRST[C_MLP] + k
                        load(u, w1[:, UNIT_KT * k:UNIT_KT * (k + 1), bass.ds(q * D + j * NW, NW)],
                             slot(u), q * (8 * UPC) + j * UPC)
                with sp.Fori(0, 4) as j:
                    for k in range(UPC):
                        u = FIRST[C_MLP + 4] + k
                        load(u, w2[:, bass.ds(q * KT + UNIT_KT * k, UNIT_KT), bass.ds(j * NW, NW)],
                             slot(u), q * (8 * UPC) + j * UPC)
            w_gate, w_proj = rows(ple_w_gate), rows(ple_w_proj)
            for n in range(4):
                u = FIRST[C_PLE + n]
                load(u, w_proj[:, :, n * NW:(n + 1) * NW], slot(u))
                for k in range(UPC):
                    load(u + 1 + k, w_gate[:, UNIT_KT * k:UNIT_KT * (k + 1), n * NW:(n + 1) * NW],
                         slot(u + 1 + k))
            out_v = out[0].rearrange("(t p) d -> p t d", p=P)
            for n, (t, at, cols) in enumerate(OUT_BLOCKS):
                sp.wait_ge(out_ready, n + 1)
                sp.dma_start(out_v[:, t, at:at + cols], h[:, t, at:at + cols]).then_inc(out_stored, 16)
            sp.wait_ge(out_stored, 16 * len(OUT_BLOCKS))

        @block.gpsimd
        def _(pool):
            nc.gpsimd.memset(ident[:], 0.0)
            nc.gpsimd.memset(causal[:], 0.0)
            nc.gpsimd.memset(cmp_neg[:], 0.0)
            nc.gpsimd.memset(cmp_one[:], 1.0)
            nc.gpsimd.memset(minus_half[:], -0.5).then_inc(set_up, 1)
            pool.wait_ge(set_up, 1)
            nc.gpsimd.affine_select(out=ident[:], in_=ident[:], compare_op=ALU.not_equal, fill=1.0, base=0,
                                    pattern=[[-1, P]], channel_multiplier=1).then_inc(set_up, 1)
            nc.gpsimd.affine_select(out=causal[:, P:], in_=causal[:, P:], compare_op=ALU.is_ge, fill=NEG,
                                    base=0, pattern=[[-1, P]], channel_multiplier=1)
            for m, fill in ((cmp_neg, NEG), (cmp_one, 0.0)):
                last = nc.gpsimd.affine_select(out=m[:], in_=m[:], compare_op=ALU.is_ge, fill=fill,
                                               base=1 - CL, pattern=[[P, TT], [-16, N_CMP]],
                                               channel_multiplier=1)
            last.then_inc(set_up, 1)

            def power(n, rows, cols, dst=None):
                pool.wait_ge(ms_ready, n + 1)
                o = rs8[0:rows, 0:cols] if dst is None else dst
                nc.gpsimd.tensor_tensor(o, ms[0:rows, 0:cols], minus_half[0:rows, 0:cols],
                                        ALU.pow).then_inc(rs_ready, 1)

            power(0, P, TT, rstd[:, 0])
            power(1, P, 8)
            power(2, P, 8)
            power(3, N_CMP, G)
            for g in range(G):
                power(4 + g, P, 8)
            power(8, P, TT, rstd[:, 1])

            def square(c, i=0):
                for t in range(TT):
                    pool.wait_ge(acc_read[c % 2][t], c // 2 + 1 + 4 * i)
                    nc.gpsimd.tensor_tensor(stage[:, t], stage[:, t], stage[:, t], ALU.mult)\
                      .then_inc(squared, 1)

            with pool.Fori(0, QUARTERS) as q:
                for j in range(4):
                    square(C_MLP + j, q)
            power(9, P, TT, rstd[:, 2])

        @block.scalar
        def _(act):
            act.wait_ge(set_up, 1)
            nc.scalar.activation(junk_act[:, 0:8], minus_half[:], ACT.Exp)
            steps = [0]

            def link(ins):
                steps[0] += 1
                ins.then_inc(act_step, 1)
                act.wait_ge(act_step, steps[0])

            def split_hi(first, n, i=0, width=UW):
                for k in range(n):
                    u = first + k
                    act.wait_ge(raw_full[u % RAW], 16 * (u // RAW + 1) + 16 * UPC * i)
                    if not (isinstance(i, int) and u < SPLIT):
                        act.wait_ge(unit_used, u - SPLIT + 1 + 8 * UPC * i)
                    nc.scalar.activation(w_hi[:, u % SPLIT, 0:width], w_raw[:, u % RAW, 0:width],
                                         ACT.Copy).then_inc(hi_done, 1)
                    yield k

            def evac(c, dst, func=ACT.Copy, scale=1.0, i=0):
                act.wait_ge(unit_used, END[c] + 8 * UPC * i)
                for t in range(TT):
                    nc.scalar.activation(dst(t), acc[c % 2][t][:], func, scale=scale[:, t:t + 1])\
                      .then_inc(acc_read[c % 2][t], 1)

            def transposed_hi(r, dst_hi, kt0, gain, i=0, banks=(0, 1)):
                for b in banks:
                    act.wait_ge(tr_full[b], r + 1 + 4 * i)
                    if gain is None:
                        last = nc.scalar.activation(
                            dst_hi[:, kt0 + 2 * b:kt0 + 2 * b + 2].rearrange("p k s -> p (k s)"), tr[b][:], ACT.Copy)
                    else:
                        for m in range(2):
                            kt = kt0 + 2 * b + m
                            last = nc.scalar.activation(dst_hi[:, kt], tr[b][:, m * SEQ:(m + 1) * SEQ], ACT.Copy,
                                                        scale=const_t[:, gain + kt:gain + kt + 1])
                    last.then_inc(tr_hi[b], 1)

            def sum_squares(norm, n):
                for t in range(TT):
                    ins = nc.scalar.activation(junk_act[:], h[:, t, n * NW:(n + 1) * NW], ACT.Square,
                                               accum_out=ss[:, norm, t, n:n + 1])
                    if n == 3 and t == TT - 1:
                        ins.then_inc(sums_ready, 1)
                        act.wait_ge(sums_ready, norm + 1)
                    else:
                        link(ins)

            def h_chunk_stats(c, norm, n):
                for t in range(TT):
                    act.wait_ge(acc_read[c % 2][t], c // 2 + 1)
                sum_squares(norm, n)

            def pos_part(kv, half):
                if half:
                    for b in range(2):
                        act.wait_ge(tr_done[b], R_KC + kv + 1)
                else:
                    act.wait_ge(pos_added, kv + 1)
                nc.scalar.activation(flat(b_hi, 8 * kv + 4 * half, 4), junk[:], ACT.Copy).then_inc(pos_hi, 1)

            def hidden(kv):
                act.wait_ge(unit_used, CMP_FIRST[kv] + CMP_UNITS)
                if kv:
                    act.wait_ge(hid_ready, kv)
                nc.scalar.activation(hid_e[:], sc[0][0:HID, 0:DK], ACT.Exp, scale=-1.0).then_inc(hid_exp, 1)

            def head_exp(hh):
                par = hh % 2
                act.wait_ge(s_read, hh + 1)
                for t in range(TT):
                    for br in range(2):
                        s = (s1 if t else s0)[:, par, br]
                        last = nc.scalar.activation(s, s, ACT.Exp, bias=nmx[:, par, 2 * t + br:2 * t + br + 1],
                                                    scale=SCALE, accum_out=sm[:, par, 2 * t + br:2 * t + br + 1])
                last.then_inc(s_exp, 1)

            def head_pt(hh):
                act.wait_ge(tr_full[0], p_set(hh) + 1)
                if hh >= 2:
                    act.wait_ge(o_full, hh - 1)
                nc.scalar.activation(p_t[:, hh % 2, 0:NW], tr[0][:], ACT.Copy).then_inc(tr_done[0], 1)

            def head_o(hh):
                act.wait_ge(o_full, hh + 1)
                nc.scalar.activation(b_hi[:, hh], out_bank(hh)[:, 0:SEQ], ACT.Copy).then_inc(o_hi, 1)

            def cmp_softmax(g):
                act.wait_ge(cmp_read, g + 1)
                nc.scalar.activation(cmp_s[:], cmp_s[:], ACT.Exp, scale=SCALE).then_inc(cmp_exp, 1)

            def to_stage(c, scale):
                evac(c, lambda t: stage[:, t], scale=scale)

            act.wait_ge(consts_ready, 1)
            transposed_hi(R_X, a_hi, 0, GAIN_MIX, banks=(0,))
            for k in split_hi(FIRST[C_KC], UPC):
                if k == 0:
                    transposed_hi(R_X, a_hi, 0, GAIN_MIX, banks=(1,))
                if k in (2, 3, 5):
                    n = (k + 1) // 2
                    transposed_hi(R_X + n, a_hi, 4 * n, GAIN_MIX)
                if k >= 4:
                    n = k - 4
                    for piece in (n + 1,) if n else (0, 1):
                        act.wait_ge(x_full[piece], 16)
                    sum_squares(0, n)
            for k in split_hi(FIRST[C_VC], UPC):
                if k == 2:
                    act.wait_ge(rs_ready, 1)
                    to_stage(C_KC, rstd[:, 0])
                if k >= 6:
                    pos_part(0, k - 6)
            for k in split_hi(FIRST[C_KS], UPC):
                if k == 2:
                    act.wait_ge(tr_full[1], R_KC + 1)
                    to_stage(C_VC, rstd[:, 0])
                if k >= 6:
                    pos_part(1, k - 6)
            for k in split_hi(CMP_FIRST[0], CMP_UNITS):
                pass
            for k in split_hi(FIRST[C_KW], UPC):
                if k == 0:
                    act.wait_ge(tr_full[1], R_VC + 1)
                    to_stage(C_KS, rstd[:, 0])
                if k == 3:
                    hidden(0)
            for k in split_hi(CMP_FIRST[1], CMP_UNITS):
                pass
            for k in split_hi(FIRST[C_VS], UPC):
                if k == 0:
                    act.wait_ge(tr_full[1], R_KS + 1)
                    to_stage(C_KW, rstd[:, 0])
                if k == 1:
                    act.wait_ge(kc_full, 1)
                    nc.scalar.activation(kc_rows[:], sc[1][0:N_CMP, :], ACT.Copy).then_inc(kc_copied, 1)
                if k == 3:
                    hidden(1)
            for k in split_hi(FIRST[C_VW], UPC):
                if k == 2:
                    evac(C_VS, lambda t: v_slc[:, t], scale=rstd[:, 0])
                if k == 3:
                    act.wait_ge(vc_full, 1)
                    nc.scalar.activation(v_cmp[:], sc[0][0:N_CMP, :], ACT.Copy).then_inc(vc_ready, 1)
                if k == 6:
                    for b in range(2):
                        act.wait_ge(tr_full[b], R_P + 1)
                        nc.scalar.activation(pt_hi[:, b], tr[b][:, 0:SEQ], ACT.Copy).then_inc(tr_hi[b], 1)
            for k in split_hi(FIRST[C_GATE], 1, width=KT * GATES):
                pass
            for k in split_hi(FIRST[C_Q], UPC):
                if k == 1:
                    evac(C_VW, lambda t: v_win[:, t], scale=rstd[:, 0])
                if k == 2:
                    act.wait_ge(unit_used, END[C_GATE])
                    for t in range(TT):
                        toks = slice(t * P, (t + 1) * P)
                        nc.scalar.activation(gate_rows[:, toks], acc[C_GATE % 2][0][0:GATES, toks], ACT.Copy)\
                          .then_inc(acc_read[C_GATE % 2][t], 1)
                if k == 6:
                    act.wait_ge(gates_full, 1)
                    act.wait_ge(neg_ready, 1)
                    for t in range(TT):
                        nc.scalar.activation(gates[:, t], sc[1][:, t * GATES:(t + 1) * GATES], ACT.Exp,
                                             scale=neg_rstd[:, t:t + 1]).then_inc(gates_exp, 1)
            for g in range(G + 1):
                first = FIRST[C_Q + g + 1] if g < G else FIRST[C_OUT] + UPC
                for k in split_hi(first, UPC):
                    n = HPG * (g - 1)
                    if k == 0 and g:
                        head_pt(n)
                        head_exp(n + 1)
                    if k == 1 and g:
                        head_o(n)
                    if k == 2:
                        if g < G:
                            act.wait_ge(tr_full[1], q_set(g - 1) + 1 if g else R_KW + 1)
                            to_stage(C_Q + g, rstd[:, 0])
                        if g:
                            head_pt(n + 1)
                            head_exp(n + 2)
                    if k == 3 and g:
                        head_o(n + 1)
                    if k == 4 and g:
                        head_pt(n + 2)
                        head_exp(n + 3)
                    if k == 5:
                        if g:
                            head_o(n + 2)
                        if g < G:
                            cmp_softmax(g)
                    if k == 6:
                        if g:
                            head_pt(n + 3)
                        if g < G:
                            head_exp(n + 4)
                    if k == 7 and g:
                        head_o(n + 3)
            for k in split_hi(FIRST[C_OUT + 2], UPC):
                if k in (1, 2):
                    h_chunk_stats(C_OUT + k - 1, 1, k - 1)
                if k in (4, 6):
                    n = k // 2 - 2
                    transposed_hi(R_H1 + n, a_hi, 4 * n, GAIN_MLP)
            for k in split_hi(FIRST[C_OUT + 3], UPC):
                if k == 2:
                    h_chunk_stats(C_OUT + 2, 1, 2)
                if k == 4:
                    transposed_hi(R_H1 + 2, a_hi, 8, GAIN_MLP)
            for k in split_hi(FIRST[C_MLP], UPC):
                if k == 2:
                    h_chunk_stats(C_OUT + 3, 1, 3)
                if k == 4:
                    transposed_hi(R_H1 + 3, a_hi, 12, GAIN_MLP)
            act.wait_ge(rs_ready, 9)

            def hidden_chunks(chunks, i):
                for j in chunks:
                    for k in split_hi(FIRST[C_MLP + j], UPC, i):
                        if k == 2:
                            evac(C_MLP + j - 1, lambda t: stage[:, t], ACT.Relu, rstd[:, 1], i)
                        if k == 4:
                            transposed_hi(R_MLP + j - 1, b_hi, 4 * (j - 1), None, i)

            with act.Fori(0, QUARTERS - 1) as q:
                hidden_chunks(range(1, 5), q)
                for j in range(5, 9):
                    for k in split_hi(FIRST[C_MLP + j], UPC, q):
                        pass
            last_q = QUARTERS - 1
            hidden_chunks(range(1, 5), last_q)
            for n in range(4):
                c = C_MLP + 8 * last_q + 4 + n
                first = FIRST[c + 1]
                for k in split_hi(first, UPC + 1 if n == 3 else UPC):
                    if k == 2:
                        h_chunk_stats(c, 2, n)
                    if k == 4:
                        transposed_hi(R_H2 + n, a_hi, 4 * n, GAIN_PLE)
            act.wait_ge(rs_ready, 10)

            def gate(n, t, at=0, cols=NW):
                c = C_PLE + n
                nc.scalar.activation(stage[:, t, at:at + cols], acc[c % 2][t][:, at:at + cols], ACT.Sigmoid,
                                     scale=rstd[:, 2, t:t + 1]).then_inc(acc_read[c % 2][t], 1)

            for n in range(4):
                if n < 3:
                    for k in split_hi(FIRST[C_PLE + n + 1], UPC + 1):
                        if k == 2:
                            act.wait_ge(unit_used, END[C_PLE + n])
                            if n:
                                act.wait_ge(out_ready, TT * n)
                            for t in range(TT):
                                gate(n, t)
                else:
                    act.wait_ge(tile_complete, 1)
                    act.wait_ge(out_ready, TT * n)
                    gate(n, 0)
                    act.wait_ge(unit_used, END[C_PLE + n])
                    for m in range(2):
                        gate(n, 1, m * (NW // 2), NW // 2)

        @block.vector
        def _(dve):
            steps = [0]

            def link(ins):
                steps[0] += 1
                ins.then_inc(dve_step, 1)
                dve.wait_ge(dve_step, steps[0])

            def split_lo(first, n, i=0, width=UW):
                for k in range(n):
                    u = first + k
                    dve.wait_ge(hi_done, u + 1 + 8 * UPC * i)
                    nc.vector.tensor_tensor(w_lo[:, u % SPLIT, 0:width], w_raw[:, u % RAW, 0:width],
                                            f32(w_hi[:, u % SPLIT, 0:width]), ALU.subtract).then_inc(lo_done, 1)
                    yield k

            def transposed_lo(r, hi, lo, kt0, gain, i=0, banks=(0, 1)):
                for b in banks:
                    dve.wait_ge(tr_hi[b], hi_sets(r) + 4 * i)
                    if gain is None:
                        last = nc.vector.tensor_tensor(
                            flat(lo, kt0 + 2 * b, 2), tr[b][:], f32(flat(hi, kt0 + 2 * b, 2)), ALU.subtract)
                    else:
                        for m in range(2):
                            kt = kt0 + 2 * b + m
                            last = nc.vector.scalar_tensor_tensor(
                                out=lo[:, kt], in0=tr[b][:, m * SEQ:(m + 1) * SEQ],
                                scalar=const_t[:, gain + kt:gain + kt + 1], in1=f32(hi[:, kt]),
                                op0=ALU.mult, op1=ALU.subtract)
                    last.then_inc(tr_done[b], 1)

            def mean_square(n, norm):
                dve.wait_ge(sums_ready, norm + 1)
                link(nc.vector.reduce_sum(head_sums[:, 0:TT], ss[:, norm], axis=AXX))
                if n:
                    dve.wait_ge(rs_ready, n)
                nc.vector.tensor_scalar(ms[:, 0:TT], head_sums[:, 0:TT], 1.0 / D, EPS, ALU.mult,
                                        ALU.add).then_inc(ms_ready, 1)

            def heads_mean_square(n, src, squares, rows, cols):
                link(nc.vector.tensor_tensor(squares, src, src, ALU.mult))
                link(nc.vector.reduce_sum(head_sums[0:rows, 0:cols], squares, axis=AXX))
                dve.wait_ge(rs_ready, n)
                nc.vector.tensor_scalar(ms[0:rows, 0:cols], head_sums[0:rows, 0:cols], 1.0 / DK, EPS,
                                        ALU.mult, ALU.add).then_inc(ms_ready, 1)

            def heads_scale(n, src, rows, cols, done):
                dve.wait_ge(rs_ready, n + 1)
                nc.vector.tensor_tensor(src, src, rs8[0:rows, 0:cols, None].to_broadcast([rows, cols, DK]),
                                        ALU.mult).then_inc(done, 1)

            stage_v = stage[:].rearrange("p t (a d) -> p (t a) d", d=DK)
            junk_v = junk[:].rearrange("p (a d) -> p a d", d=DK)
            kc_v = kc_rows[:].rearrange("p (a d) -> p a d", d=DK)
            kc_sq_v = kc_sq[:].rearrange("p (a d) -> p a d", d=DK)

            def staged_mean_square(n, c):
                for t in range(TT):
                    dve.wait_ge(acc_read[c % 2][t], c // 2 + 1)
                heads_mean_square(n, stage_v, junk_v, P, TT * HPG)

            def staged_scale(n):
                heads_scale(n, stage_v, P, TT * HPG, normed)

            def keys_out(r, br):
                for b in range(2):
                    dve.wait_ge(tr_full[b], r + 1)
                    nc.vector.tensor_scalar(k_t[:, 2 * b:2 * b + 2, :, br],
                                            tr[b][:].rearrange("p (g t s) -> p g t s", g=2, t=TT),
                                            const_t[:, GAIN_K + 1 + br:GAIN_K + 2 + br], None, ALU.mult)\
                      .then_inc(tr_done[b], 1)

            def queries_out(g):
                for b in range(2):
                    dve.wait_ge(tr_full[b], q_set(g) + 1)
                    nc.vector.tensor_scalar(q_t[:, 2 * b:2 * b + 2], tr[b][:].rearrange("p (m s) -> p m s", m=2),
                                            const_t[:, GAIN_Q:GAIN_Q + 1], None, ALU.mult).then_inc(tr_done[b], 1)

            def pos_part(kv, half):
                r = R_KC + kv
                for b in range(2):
                    if not half:
                        dve.wait_ge(tr_full[b], r + 1)
                    col = POS + kv * CL + half * (CL // 2)
                    ins = nc.vector.tensor_tensor(
                        junk[:, b * NW:(b + 1) * NW].rearrange("p (m l) -> p m l", l=CL // 2),
                        tr[b][:].rearrange("p (m l) -> p m l", l=CL // 2),
                        const_t[:, None, col:col + CL // 2].to_broadcast([P, NW // (CL // 2), CL // 2]), ALU.add)
                    if half:
                        ins.then_inc(tr_done[b], 1)
                    elif b:
                        ins.then_inc(pos_added, 1)
                dve.wait_ge(pos_hi, 2 * kv + half + 1)
                kt0 = 8 * kv + 4 * half
                ins = nc.vector.tensor_tensor(flat(b_lo, kt0, 4), junk[:], f32(flat(b_hi, kt0, 4)), ALU.subtract)
                ins.then_inc(pos_split, 1)
                dve.wait_ge(pos_split, 2 * kv + half + 1)

            def hidden(kv):
                dve.wait_ge(hid_exp, kv + 1)
                if kv:
                    dve.wait_ge(kc_full, 1)
                link(nc.vector.tensor_scalar(hid_e[:], hid_e[:], 1.0, None, ALU.add))
                link(nc.vector.reciprocal(hid_e[:], hid_e[:]))
                nc.vector.tensor_tensor(hid_rows[:], sc[0][0:HID, 0:DK], hid_e[:], ALU.mult).then_inc(hid_ready, 1)

            def hidden_out(kv):
                dve.wait_ge(hid_full, kv + 1)
                nc.vector.tensor_copy(hid[:], sc[1][:, 0:HID]).then_inc(hid_copied, 1)

            def head_max(hh):
                par = hh % 2
                dve.wait_ge(s_full, hh + 1)
                for t in range(TT):
                    for br in range(2):
                        if t:
                            scores = sc[1][:].rearrange("p (t b s) -> p t b s", t=TT, b=2)[:, :, br]
                            masked = s1[:, par, br].rearrange("p (t s) -> p t s", t=TT)
                            mask = causal[:].rearrange("p (t s) -> p t s", t=TT)
                        else:
                            scores, masked, mask = sc[0][:, br * P:(br + 1) * P], s0[:, par, br], causal[:, P:]
                        m = 2 * t + br
                        ins = nc.vector.tensor_tensor_reduce(out=masked, in0=scores, in1=mask, scale=1.0,
                                                             scalar=-3e38, op0=ALU.add, op1=ALU.max,
                                                             accum_out=mx[:, par, m:m + 1])
                link(ins)
                nc.vector.tensor_scalar(nmx[:, par], mx[:, par], -SCALE, None, ALU.mult).then_inc(s_read, 1)

            def head_scale(hh):
                par = hh % 2
                dve.wait_ge(s_exp, hh + 1)
                link(nc.vector.tensor_scalar(sm[:, par], sm[:, par], 1e-30, None, ALU.max))
                link(nc.vector.reciprocal(cf[:, par], sm[:, par]))
                c4 = cf[:, par].rearrange("p (t b) -> p t b", t=TT)
                link(nc.vector.tensor_tensor(c4, c4, gates[:, :, 3 * hh + 1:3 * hh + 3], ALU.mult))
                for t in range(TT):
                    for br in range(2):
                        s = (s1 if t else s0)[:, par, br]
                        ins = nc.vector.tensor_scalar(s, s, cf[:, par, 2 * t + br:2 * t + br + 1], None, ALU.mult)
                ins.then_inc(s_scaled, 1)

            def cmp_max(g):
                dve.wait_ge(cmp_full, g + 1)
                scores = sc[1][:, 0:TT * HPG * N_CMP].rearrange("p (t j n) -> p t j n", t=TT, j=HPG)
                link(nc.vector.tensor_tensor(cmp_s[:], scores,
                                             cmp_neg[:, :, None, :].to_broadcast([P, TT, HPG, N_CMP]), ALU.add))
                rows = cmp_s[:].rearrange("p t j n -> p (t j) n")
                link(nc.vector.reduce_max(cmp_m[:], rows, axis=AXX))
                nc.vector.tensor_tensor(rows, rows, cmp_m[:, :, None].to_broadcast([P, TT * HPG, N_CMP]),
                                        ALU.subtract).then_inc(cmp_read, 1)

            def cmp_scale(g):
                dve.wait_ge(cmp_exp, g + 1)
                link(nc.vector.tensor_tensor(cmp_s[:], cmp_s[:],
                                             cmp_one[:, :, None, :].to_broadcast([P, TT, HPG, N_CMP]), ALU.mult))
                rows = cmp_s[:].rearrange("p t j n -> p (t j) n")
                link(nc.vector.reduce_sum(cmp_c[:], rows, axis=AXX))
                link(nc.vector.tensor_scalar(cmp_c[:], cmp_c[:], 1e-30, None, ALU.max))
                link(nc.vector.reciprocal(cmp_c[:], cmp_c[:]))
                c8 = cmp_c[:].rearrange("p (t j) -> p t j", t=TT)
                own = gates[:, :, 3 * HPG * g:3 * HPG * (g + 1)].rearrange("p t (j b) -> p t j b", b=3)[:, :, :, 0]
                link(nc.vector.tensor_tensor(c8, c8, own, ALU.mult))
                nc.vector.tensor_tensor(cmp_p[:, g % 2].rearrange("p t j n -> p (t j) n"), rows,
                                        cmp_c[:, :, None].to_broadcast([P, TT * HPG, N_CMP]),
                                        ALU.mult).then_inc(cmp_ready, 1)

            def head_pt(hh):
                dve.wait_ge(tr_full[1], p_set(hh) + 1)
                if hh >= 2:
                    dve.wait_ge(o_full, hh - 1)
                nc.vector.tensor_copy(p_t[:, hh % 2, NW:NW + SEQ], tr[1][:, 0:SEQ])
                nc.vector.tensor_copy(p_t[0:N_CMP, hh % 2, NW + SEQ:2 * NW], tr[1][0:N_CMP, SEQ:NW])\
                  .then_inc(tr_done[1], 1)

            def head_o(hh):
                dve.wait_ge(o_hi, hh + 1)
                nc.vector.tensor_tensor(b_lo[:, hh], out_bank(hh)[:, 0:SEQ], f32(b_hi[:, hh]), ALU.subtract)\
                  .then_inc(o_done, 1)

            def add_to_h(c, n, i=0):
                dve.wait_ge(unit_used, END[c] + 8 * UPC * i)
                for t in range(TT):
                    cols = h[:, t, n * NW:(n + 1) * NW]
                    nc.vector.tensor_tensor(cols, acc[c % 2][t][:], cols, ALU.add).then_inc(acc_read[c % 2][t], 1)

            def constants(n, at, cols):
                dve.wait_ge(consts_in_psum, n)
                nc.vector.tensor_copy(const_t[:, at:at + cols], sc[0][:, at:at + cols]).then_inc(consts_ready, 1)
                dve.wait_ge(consts_ready, n)

            constants(1, 0, KT)
            transposed_lo(R_X, a_hi, a_lo, 0, GAIN_MIX, banks=(0,))
            for k in split_lo(FIRST[C_KC], UPC):
                if k == 0:
                    transposed_lo(R_X, a_hi, a_lo, 0, GAIN_MIX, banks=(1,))
                if k in (2, 3, 5):
                    n = (k + 1) // 2
                    transposed_lo(R_X + n, a_hi, a_lo, 4 * n, GAIN_MIX)
            for k in split_lo(FIRST[C_VC], UPC):
                if k == 0:
                    mean_square(0, 0)
                if k == 1:
                    dve.wait_ge(rs_ready, 1)
                    nc.vector.tensor_scalar(neg_rstd[:], rstd[:, 0], -1.0, None, ALU.mult).then_inc(neg_ready, 1)
                if k == 3:
                    constants(2, KT, N_CONST - KT)
                    dve.wait_ge(set_up, 3)
                if k >= 6:
                    pos_part(0, k - 6)
            for k in split_lo(FIRST[C_KS], UPC):
                if k >= 6:
                    pos_part(1, k - 6)
            for k in split_lo(CMP_FIRST[0], CMP_UNITS):
                pass
            for k in split_lo(FIRST[C_KW], UPC):
                if k == 0:
                    staged_mean_square(1, C_KS)
                if k == 1:
                    staged_scale(1)
                if k == 3:
                    hidden(0)
                if k == 5:
                    hidden_out(0)
                if k == 6:
                    keys_out(R_KS, 0)
            for k in split_lo(CMP_FIRST[1], CMP_UNITS):
                pass
            for k in split_lo(FIRST[C_VS], UPC):
                if k == 0:
                    staged_mean_square(2, C_KW)
                if k == 1:
                    staged_scale(2)
                if k == 2:
                    dve.wait_ge(kc_copied, 1)
                    heads_mean_square(3, kc_v, kc_sq_v, N_CMP, G)
                if k == 3:
                    heads_scale(3, kc_v, N_CMP, G, kc_normed)
                    hidden(1)
                if k == 5:
                    hidden_out(1)
                if k == 6:
                    keys_out(R_KW, 1)
            for k in split_lo(FIRST[C_VW], UPC):
                if k == 1:
                    dve.wait_ge(kct_full, 1)
                    nc.vector.tensor_scalar(kc_t[:].rearrange("p g n -> p (g n)"), sc[1][:, 0:G * N_CMP],
                                            const_t[:, GAIN_K:GAIN_K + 1], None, ALU.mult).then_inc(kct_ready, 1)
                if k == 6:
                    for b in range(2):
                        dve.wait_ge(tr_hi[b], hi_sets(R_P))
                        nc.vector.tensor_tensor(pt_lo[:, b], tr[b][:, 0:SEQ], f32(pt_hi[:, b]), ALU.subtract)\
                          .then_inc(tr_done[b], 1)
            for k in split_lo(FIRST[C_GATE], 1, width=KT * GATES):
                pass
            for k in split_lo(FIRST[C_Q], UPC):
                if k == 7:
                    dve.wait_ge(gates_exp, TT)
                    link(nc.vector.tensor_scalar(gates[:], gates[:], 1.0, None, ALU.add))
                    link(nc.vector.reciprocal(gates[:], gates[:]))
            for g in range(G + 1):
                first = FIRST[C_Q + g + 1] if g < G else FIRST[C_OUT] + UPC
                for k in split_lo(first, UPC):
                    n = HPG * (g - 1)
                    if k == 0 and g:
                        head_max(n + 1)
                        head_pt(n)
                    if k == 1 and g:
                        head_scale(n + 1)
                        head_o(n)
                    if k == 2:
                        if g:
                            head_max(n + 2)
                            head_pt(n + 1)
                        if g < G:
                            staged_mean_square(4 + g, C_Q + g)
                    if k == 3:
                        if g:
                            head_scale(n + 2)
                            head_o(n + 1)
                        if g < G:
                            staged_scale(4 + g)
                    if k == 4:
                        if g:
                            head_max(n + 3)
                            head_pt(n + 2)
                        if g < G:
                            queries_out(g)
                    if k == 5:
                        if g:
                            head_scale(n + 3)
                        if g:
                            head_o(n + 2)
                        if g < G:
                            cmp_max(g)
                    if k == 6:
                        if g < G:
                            head_max(n + 4)
                        if g:
                            head_pt(n + 3)
                        if g < G:
                            cmp_scale(g)
                    if k == 7:
                        if g < G:
                            head_scale(n + 4)
                        if g:
                            head_o(n + 3)
            for piece in range(5):
                dve.wait_ge(x_full[piece], 16)
            for k in split_lo(FIRST[C_OUT + 2], UPC):
                if k in (1, 2):
                    add_to_h(C_OUT + k - 1, k - 1)
                if k in (4, 6):
                    n = k // 2 - 2
                    transposed_lo(R_H1 + n, a_hi, a_lo, 4 * n, GAIN_MLP)
            for k in split_lo(FIRST[C_OUT + 3], UPC):
                if k == 2:
                    add_to_h(C_OUT + 2, 2)
                if k == 4:
                    transposed_lo(R_H1 + 2, a_hi, a_lo, 8, GAIN_MLP)
            for k in split_lo(FIRST[C_MLP], UPC):
                if k == 2:
                    add_to_h(C_OUT + 3, 3)
                if k == 3:
                    mean_square(8, 1)
                if k == 4:
                    transposed_lo(R_H1 + 3, a_hi, a_lo, 12, GAIN_MLP)

            def hidden_chunks(i):
                for j in range(1, 5):
                    for k in split_lo(FIRST[C_MLP + j], UPC, i):
                        if k == 4:
                            transposed_lo(R_MLP + j - 1, b_hi, b_lo, 4 * (j - 1), None, i)

            with dve.Fori(0, QUARTERS - 1) as q:
                hidden_chunks(q)
                for j in range(5, 9):
                    for k in split_lo(FIRST[C_MLP + j], UPC, q):
                        if k == 2:
                            add_to_h(C_MLP + j - 1, j - 5, q)
            last_q = QUARTERS - 1
            hidden_chunks(last_q)
            for n in range(4):
                c = C_MLP + 8 * last_q + 4 + n
                for k in split_lo(FIRST[c + 1], UPC + 1 if n == 3 else UPC):
                    if k == 2:
                        add_to_h(c, n)
                    if k == 3 and n == 3:
                        mean_square(9, 2)
                    if k == 4:
                        transposed_lo(R_H2 + n, a_hi, a_lo, 4 * n, GAIN_PLE)

            def gated_out(n, t, at=0, cols=NW, part=0):
                c = C_PLE + n
                dve.wait_ge(acc_read[c % 2][t], c // 2 + 1 + part)
                own = stage[:, t, at:at + cols]
                link(nc.vector.tensor_tensor(own, (tr if n % 2 else sc)[t][:, at:at + cols], own, ALU.mult))
                res = h[:, t, n * NW + at:n * NW + at + cols]
                nc.vector.tensor_tensor(res, own, res, ALU.add).then_inc(out_ready, 1)

            for n in range(3):
                for k in split_lo(FIRST[C_PLE + n + 1], UPC + 1):
                    if k == 2:
                        for t in range(TT):
                            gated_out(n, t)
            gated_out(3, 0)
            for m in range(2):
                gated_out(3, 1, m * (NW // 2), NW // 2, m)

        @block.tensor
        def _(pe):
            def bank_free(c, i=0):
                if c >= 2:
                    for t in range(TT):
                        pe.wait_ge(acc_read[c % 2][t], c // 2 + 4 * i)

            def tile_product(c, u, kt, t, x_hi, x_lo):
                m, toks = kt % UNIT_KT, slice(t * P, (t + 1) * P)
                for n, (xs, ws) in enumerate(((x_hi, w_hi), (x_hi, w_lo), (x_lo, w_hi))):
                    last = nc.tensor.matmul(acc[c % 2][t][:], xs[:, kt, toks],
                                            ws[:, u % SPLIT, m * NW:(m + 1) * NW],
                                            start=(kt == 0 and n == 0), stop=(kt == KT - 1 and n == 2))
                return last

            def half_unit(c, u, kt, x_hi, x_lo, i=0):
                k, m = divmod(kt, UNIT_KT)
                if kt == 0:
                    bank_free(c, i)
                if m == 0:
                    pe.wait_ge(lo_done, u + 1 + 8 * UPC * i)
                for t in range(TT):
                    last = tile_product(c, u, kt, t, x_hi, x_lo)
                if m == UNIT_KT - 1:
                    last.then_inc(unit_used, 1)

            def unit(c, u, k, x_hi, x_lo, i=0):
                for m in range(UNIT_KT):
                    half_unit(c, u, UNIT_KT * k + m, x_hi, x_lo, i)

            def gate_unit(c, u):
                bank_free(c)
                pe.wait_ge(lo_done, u + 1)
                for kt in range(KT):
                    for n, (xs, ws) in enumerate(((a_hi, w_hi), (a_hi, w_lo), (a_lo, w_hi))):
                        last = nc.tensor.matmul(acc[c % 2][0][0:GATES, 0:SEQ],
                                                ws[:, u % SPLIT, kt * GATES:(kt + 1) * GATES], xs[:, kt],
                                                start=(kt == 0 and n == 0), stop=(kt == KT - 1 and n == 2))
                last.then_inc(unit_used, 1)

            def ple_unit(n, u):
                banks = tr if n % 2 else sc
                if n >= 2:
                    pe.wait_ge(out_ready, TT * (n - 1))
                pe.wait_ge(lo_done, u + 1)
                for t in range(TT):
                    for kt in range(PLE // P):
                        toks = slice(t * P, (t + 1) * P)
                        for m, (xs, ws) in enumerate(((pt_hi, w_hi), (pt_hi, w_lo), (pt_lo, w_hi))):
                            last = nc.tensor.matmul(banks[t][:], xs[:, kt, toks],
                                                    ws[:, u % SPLIT, kt * NW:(kt + 1) * NW],
                                                    start=(kt == 0 and m == 0), stop=(kt == 1 and m == 2))
                last.then_inc(unit_used, 1)

            def transpose_bank(r, b, src, i=0):
                if r:
                    pe.wait_ge(tr_done[b], r + 4 * i)
                for m in range(2):
                    for t in range(TT):
                        last = nc.tensor.transpose(tr[b][:, m * SEQ + t * P:m * SEQ + (t + 1) * P],
                                                   src(t, 2 * b + m), ident[:])
                last.then_inc(tr_full[b], 1)

            def transpose_set(r, src, i=0):
                for b in range(2):
                    transpose_bank(r, b, src, i)

            def from_stage(t, b):
                return stage[:, t, b * P:(b + 1) * P]

            def from_h(n):
                return lambda t, b: h[:, t, n * NW + b * P:n * NW + (b + 1) * P]

            def staged(c):
                for t in range(TT):
                    pe.wait_ge(acc_read[c % 2][t], c // 2 + 1)

            def split_by(r, k, i=0):
                pe.wait_ge(tr_done[k % 2], r + k // 2 + 1 + 4 * i)

            def compress(kv):
                pe.wait_ge(pos_split, 2 * (kv + 1))
                if kv:
                    pe.wait_ge(hid_ready, 1)
                per = CL // CMP_UNITS
                for k in range(CMP_UNITS):
                    u = CMP_FIRST[kv] + k
                    pe.wait_ge(lo_done, u + 1)
                    for m in range(per):
                        pos = per * k + m
                        half, l = divmod(pos, CSTEP)
                        at = l + half * CSTEP
                        xh, xl = (flat(x, 8 * kv + 4 * half, 4)[:, at:at + CSTEP * (HID - 1) + 1:CSTEP]
                                  for x in (b_hi, b_lo))
                        wh, wl = (w[:, u % SPLIT, m * DK:(m + 1) * DK] for w in (w_hi, w_lo))
                        for n, (xs, ws) in enumerate(((xh, wh), (xh, wl), (xl, wh))):
                            last = nc.tensor.matmul(sc[0][0:HID, 0:DK], xs, ws, start=(pos == 0 and n == 0),
                                                    stop=(pos == CL - 1 and n == 2))
                    last.then_inc(unit_used, 1)

            def hidden_transpose(kv):
                pe.wait_ge(hid_ready, kv + 1)
                if kv:
                    pe.wait_ge(kc_copied, 1)
                nc.tensor.transpose(sc[1][:, 0:HID], hid_rows[:], ident[0:HID, 0:HID]).then_inc(hid_full, 1)

            def second_layer(kv, bank, done):
                pe.wait_ge(hid_copied, kv + 1)
                for g in range(G):
                    at = g * (N_CMP + 1)
                    last = nc.tensor.matmul(bank[0:N_CMP, g * DK:(g + 1) * DK], hid[:, at:at + N_CMP],
                                            cmp_w2[:, kv], start=True, stop=True)
                last.then_inc(done, 1)

            def head_scores(hh):
                j, g = hh % HPG, hh // HPG
                if hh:
                    pe.wait_ge(s_read, hh)
                if hh and j == 0:
                    pe.wait_ge(o_done, hh - 1)
                pe.wait_ge(cmp_read, g + 1)
                keys = k_t[:, g].rearrange("p t b s -> p (t b s)")
                nc.tensor.matmul(sc[0][:, 0:SEQ], q_t[:, j, 0:P], keys[:, 0:SEQ], start=True, stop=True)
                nc.tensor.matmul(sc[1][:], q_t[:, j, P:SEQ], keys, start=True, stop=True).then_inc(s_full, 1)

            def cmp_scores(g):
                for b in range(2):
                    pe.wait_ge(tr_done[b], q_set(g) + 1)
                if g:
                    pe.wait_ge(s_read, HPG * g)
                else:
                    pe.wait_ge(kct_ready, 1)
                    pe.wait_ge(vc_ready, 1)
                for t in range(TT):
                    for j in range(HPG):
                        at = (t * HPG + j) * N_CMP
                        last = nc.tensor.matmul(sc[1][:, at:at + N_CMP], q_t[:, j, t * P:(t + 1) * P], kc_t[:, g],
                                                start=True, stop=True)
                last.then_inc(cmp_full, 1)

            def head_transpose(hh):
                par, j, g, r = hh % 2, hh % HPG, hh // HPG, p_set(hh)
                pe.wait_ge(s_scaled, hh + 1)
                pe.wait_ge(cmp_ready, g + 1)
                pe.wait_ge(tr_done[0], r)
                if hh:
                    pe.wait_ge(o_done, hh)
                for br in range(2):
                    nc.tensor.transpose(tr[0][:, br * SEQ:br * SEQ + P], s0[:, par, br], ident[:])
                    last = nc.tensor.transpose(tr[0][:, br * SEQ + P:(br + 1) * SEQ], s1[:, par, br, 0:P], ident[:])
                last.then_inc(tr_full[0], 1)
                pe.wait_ge(tr_done[1], r)
                for br in range(2):
                    nc.tensor.transpose(tr[1][:, br * P:(br + 1) * P], s1[:, par, br, P:SEQ], ident[:])
                for t in range(TT):
                    last = nc.tensor.transpose(tr[1][0:N_CMP, SEQ + t * P:SEQ + (t + 1) * P],
                                               cmp_p[:, g % 2, t, j], ident[:])
                last.then_inc(tr_full[1], 1)

            def head_output(hh):
                par, g, r = hh % 2, hh // HPG, p_set(hh)
                for b in range(2):
                    pe.wait_ge(tr_done[b], r + 1)
                if hh % HPG == 2:
                    pe.wait_ge(s_read, hh + 2)
                cols = slice(g * DK, (g + 1) * DK)
                pt, o = p_t[:, par], out_bank(hh)[:, 0:SEQ]
                nc.tensor.matmul(o, v_slc[:, 0, cols], pt[:, 0:SEQ], start=True, stop=False)
                nc.tensor.matmul(o, v_win[:, 0, cols], pt[:, SEQ:2 * SEQ], start=False, stop=False)
                nc.tensor.matmul(o[:, P:SEQ], v_slc[:, 1, cols], pt[:, NW:NW + P], start=False, stop=False)
                nc.tensor.matmul(o[:, P:SEQ], v_win[:, 1, cols], pt[:, NW + P:NW + SEQ], start=False, stop=False)
                nc.tensor.matmul(o, v_cmp[:, cols], pt[0:N_CMP, NW + SEQ:2 * NW], start=False, stop=True)\
                  .then_inc(o_full, 1)

            def attention_step(g, s):
                n = HPG * (g - 1)
                if g:
                    if s in (0, 4):
                        head_scores(n + 2 + s // 4)
                    if s in (1, 5, 9):
                        head_transpose(n + 1 + s // 4)
                    if s in (3, 7, 11):
                        head_output(n + 1 + s // 4)
                if g < G:
                    if s == 6:
                        pe.wait_ge(normed, 3 + g)
                        transpose_set(q_set(g), from_stage)
                    if s == 7:
                        cmp_scores(g)
                    if s in (8, 12):
                        head_scores(n + 4 + (s - 8) // 4)
                    if s == 13:
                        head_transpose(n + 4)
                    if s == 15:
                        head_output(n + 4)

            def keep_busy(n):
                for _ in range(n):
                    nc.tensor.transpose(sc[1][:, 0:P], ident[:], ident[:])

            pe.wait_ge(set_up, 2)
            pe.wait_ge(mix_full, 16)
            nc.tensor.transpose(sc[0][:, 0:KT], const_rows[0:KT], ident[0:KT, 0:KT]).then_inc(consts_in_psum, 1)
            keep_busy(4)
            for b in range(2):
                pe.wait_ge(x_full[b], 16)
                transpose_bank(R_X, b, from_h(0))
            keep_busy(12)
            for k in range(UPC):
                if k in (1, 2, 4):
                    n = (k + 2) // 2
                    pe.wait_ge(x_full[n + 1], 16)
                    transpose_set(R_X + n, from_h(n))
                split_by(R_X, k)
                unit(C_KC, FIRST[C_KC] + k, k, a_hi, a_lo)
            for k in range(UPC):
                if k == 2:
                    pe.wait_ge(const_full, 16 * 5)
                    pe.wait_ge(consts_ready, 1)
                    nc.tensor.transpose(sc[0][:, 0:N_CONST], const_rows[:], ident[0:N_CONST, 0:N_CONST])\
                      .then_inc(consts_in_psum, 1)
                if k == 4:
                    staged(C_KC)
                    transpose_set(R_KC, from_stage)
                unit(C_VC, FIRST[C_VC] + k, k, a_hi, a_lo)
            for k in range(UPC):
                if k == 4:
                    staged(C_VC)
                    transpose_set(R_VC, from_stage)
                unit(C_KS, FIRST[C_KS] + k, k, a_hi, a_lo)
            pe.wait_ge(consts_ready, 2)
            compress(0)
            for k in range(UPC):
                if k == 4:
                    pe.wait_ge(normed, 1)
                    transpose_set(R_KS, from_stage)
                if k == 5:
                    hidden_transpose(0)
                if k == 6:
                    pe.wait_ge(cmp_w2_full, 16)
                    second_layer(0, sc[1], kc_full)
                unit(C_KW, FIRST[C_KW] + k, k, a_hi, a_lo)
            compress(1)
            for k in range(UPC):
                if k == 4:
                    pe.wait_ge(normed, 2)
                    transpose_set(R_KW, from_stage)
                if k == 5:
                    hidden_transpose(1)
                if k == 6:
                    second_layer(1, sc[0], vc_full)
                if k == 7:
                    pe.wait_ge(kc_normed, 1)
                    for g in range(G):
                        last = nc.tensor.transpose(sc[1][:, g * N_CMP:(g + 1) * N_CMP],
                                                   kc_rows[:, g * DK:(g + 1) * DK], ident[0:N_CMP, 0:N_CMP])
                    last.then_inc(kct_full, 1)
                unit(C_VS, FIRST[C_VS] + k, k, a_hi, a_lo)
            for k in range(UPC):
                if k == 4:
                    pe.wait_ge(p_full, 16)
                    for b in range(2):
                        pe.wait_ge(tr_done[b], R_P)
                        for t in range(TT):
                            last = nc.tensor.transpose(tr[b][:, t * P:(t + 1) * P],
                                                       p_rows[:, t, b * P:(b + 1) * P], ident[:])
                        last.then_inc(tr_full[b], 1)
                unit(C_VW, FIRST[C_VW] + k, k, a_hi, a_lo)
            gate_unit(C_GATE, FIRST[C_GATE])
            for k in range(UPC):
                if k == 4:
                    staged(C_GATE)
                    for t in range(TT):
                        last = nc.tensor.transpose(sc[1][:, t * GATES:(t + 1) * GATES],
                                                   gate_rows[:, t * P:(t + 1) * P], ident[0:GATES, 0:GATES])
                    last.then_inc(gates_full, 1)
                unit(C_Q, FIRST[C_Q] + k, k, a_hi, a_lo)
            for g in range(G - 1):
                c = C_Q + g + 1
                for s in range(KT):
                    attention_step(g, s)
                    half_unit(c, FIRST[c] + s // UNIT_KT, s, a_hi, a_lo)
            for n, (nn, k) in enumerate(pair_order()):
                for m in range(UNIT_KT):
                    s = UNIT_KT * n + m
                    attention_step(G - 1 + s // KT, s % KT)
                    pe.wait_ge(o_done, UNIT_KT * k + m + 1)
                    half_unit(C_OUT + nn, FIRST[C_OUT] + n, UNIT_KT * k + m, b_hi, b_lo)
            for n in (2, 3):
                c = C_OUT + n
                for k in range(UPC):
                    if k == 2:
                        staged(c - 2 if n == 2 else c - 1)
                        transpose_set(R_H1 + (0 if n == 2 else 2), from_h(0 if n == 2 else 2))
                    if k == 4 and n == 2:
                        staged(c - 1)
                        transpose_set(R_H1 + 1, from_h(1))
                    unit(c, FIRST[c] + k, k, b_hi, b_lo)
            for k in range(UPC):
                if k == 2:
                    staged(C_OUT + 3)
                    transpose_set(R_H1 + 3, from_h(3))
                split_by(R_H1, k)
                unit(C_MLP, FIRST[C_MLP] + k, k, a_hi, a_lo)

            def hidden_chunks(i):
                for j in range(1, 5):
                    for k in range(UPC):
                        if k == 2:
                            pe.wait_ge(squared, TT * j + 4 * TT * i)
                            transpose_set(R_MLP + j - 1, from_stage, i)
                        if j == 4:
                            split_by(R_MLP, k, i)
                        x_hi, x_lo = (b_hi, b_lo) if j == 4 else (a_hi, a_lo)
                        unit(C_MLP + j, FIRST[C_MLP + j] + k, k, x_hi, x_lo, i)

            with pe.Fori(0, QUARTERS - 1) as q:
                hidden_chunks(q)
                for j in range(5, 9):
                    x_hi, x_lo = (b_hi, b_lo) if j < 8 else (a_hi, a_lo)
                    for k in range(UPC):
                        unit(C_MLP + j, FIRST[C_MLP + j] + k, k, x_hi, x_lo, q)
            last_q = QUARTERS - 1
            hidden_chunks(last_q)
            for n in range(3):
                c = C_MLP + 8 * last_q + 5 + n
                for k in range(UPC):
                    if k == 2:
                        staged(c - 1)
                        transpose_set(R_H2 + n, from_h(n))
                    unit(c, FIRST[c] + k, k, b_hi, b_lo)
            for n in range(4):
                c = C_PLE + n
                if n == 1:
                    for b in range(2):
                        pe.wait_ge(tr_done[b], R_H2 + 4)
                ple_unit(n, FIRST[c])
                for k in range(UPC if n < 3 else UPC - LATE_UNITS):
                    if n == 0 and k == 2:
                        staged(c - 1)
                        transpose_set(R_H2 + 3, from_h(3))
                    if n == 0:
                        split_by(R_H2, k)
                    unit(c, FIRST[c] + 1 + k, k, a_hi, a_lo)
            for t in range(TT):
                for k in range(UPC - LATE_UNITS, UPC):
                    u = FIRST[c] + 1 + k
                    if t == 0:
                        pe.wait_ge(lo_done, u + 1)
                    for m in range(UNIT_KT):
                        last = tile_product(c, u, UNIT_KT * k + m, t, a_hi, a_lo)
                    if t:
                        last.then_inc(unit_used, 1)
                    elif k == UPC - 1:
                        last.then_inc(tile_complete, 1)


_INS = ['x', 'p', 'norm_mix_g', 'norm_mlp_g', 'mlp_w1', 'mlp_w2', 'ple_norm_g', 'ple_w_gate', 'ple_w_proj',
        'nsa_w_in', 'nsa_q_g', 'nsa_k_g', 'nsa_cmp_pos', 'nsa_cmp_w1', 'nsa_cmp_w2', 'nsa_w_out']


def kernel(**inputs):
    import numpy as _np
    import concourse.bacc as _bacc
    from concourse import mybir as _mybir
    from concourse.bass_utils import run_bass_kernel_spmd as _run

    nc = _bacc.Bacc("TRN2", target_bir_lowering=False, num_devices=1)
    arrays, args = {}, []
    for name in _INS:
        a = _np.ascontiguousarray(inputs[name])
        arrays[f"in_{name}_dram"] = a
        args.append(nc.dram_tensor(f"in_{name}_dram", a.shape, _mybir.dt.from_np(a.dtype), kind="ExternalInput").ap())
    o = nc.dram_tensor("out_dram", (1, SEQ, D), F32, kind="ExternalOutput").ap()
    trunk_layer(nc, *args, o)
    r = _run(nc, [arrays], core_ids=[0])
    return r.results[0]["out_dram"]
```
